# Optimizing a Trainium2 kernel written in Bass

```python
import jax, jax.numpy as jnp
from jax import lax
import numpy as np

D_MODEL = 1024
BATCH = 1
SEQ = 1024
DEPTH = 2
DEC_BATCH = 8
DEC_SEQ = 4
PAST_LEN = 1024
PAGE_SIZE = 128

N_MIXERS = 2
N_CONV_LAYERS = (DEPTH + 1) // 2
N_ATTN_LAYERS = DEPTH // 2
CONV_WIDTH = 31
CONV_HIST = CONV_WIDTH - 1
N_HEADS = 16
HEAD_DIM = D_MODEL // N_HEADS
Q_BLOCK = 128
D_FF = ((8 * D_MODEL + 3 * 256 - 1) // (3 * 256)) * 256
EPS = 1e-6
FORGET_BIAS_MEAN = 3.0

kernel_name = "conformer_conv_fox_hybrid_step"

def rmsnorm(x, g):
    xf = x.astype(jnp.float32)
    y = xf * lax.rsqrt(jnp.mean(xf * xf, axis=-1, keepdims=True) + EPS)
    return (y * g.astype(jnp.float32)).astype(x.dtype)

def layernorm(x, g, b):
    xf = x.astype(jnp.float32)
    mu = jnp.mean(xf, axis=-1, keepdims=True)
    var = jnp.mean(jnp.square(xf - mu), axis=-1, keepdims=True)
    y = (xf - mu) * lax.rsqrt(var + EPS)
    return (y * g.astype(jnp.float32) + b.astype(jnp.float32)).astype(x.dtype)

def conv_module(xn, hist, w_in, b_in, w_dw, b_dw, ln_g, ln_b, w_out, b_out):
    h = xn @ w_in + b_in
    a, gate = jnp.split(h, 2, axis=-1)
    u = a * jax.nn.sigmoid(gate)
    upad = jnp.concatenate([hist.astype(u.dtype), u], axis=1)
    y = lax.conv_general_dilated(
        upad, w_dw[:, None, :].astype(u.dtype), window_strides=(1,), padding='VALID',
        dimension_numbers=('NWC', 'WIO', 'NWC'), feature_group_count=u.shape[-1]) + b_dw
    y = jax.nn.silu(layernorm(y, ln_g, ln_b))
    out = y @ w_out + b_out
    return out, upad[:, -CONV_HIST:]

def fox_proj(xn, w_in, b_f):
    B, T, D = xn.shape
    p = xn @ w_in
    q = p[..., :D].reshape(B, T, N_HEADS, HEAD_DIM)
    k = p[..., D:2 * D].reshape(B, T, N_HEADS, HEAD_DIM)
    v = p[..., 2 * D:3 * D].reshape(B, T, N_HEADS, HEAD_DIM)
    logf = jax.nn.log_sigmoid((p[..., 3 * D:] + b_f).astype(jnp.float32))
    return q, k, v, logf

def fox_prompt(q, k, v, logf):
    B, S, H, dh = q.shape
    scale = dh ** -0.5
    c = jnp.cumsum(logf, axis=1)
    cT = jnp.transpose(c, (0, 2, 1))
    nb = S // Q_BLOCK
    qb = jnp.transpose(q.reshape(B, nb, Q_BLOCK, H, dh), (1, 0, 2, 3, 4))
    cqb = jnp.transpose(c.reshape(B, nb, Q_BLOCK, H), (1, 0, 3, 2))
    kpos = jnp.arange(S)

    def block(args):
        i, qi, ci = args
        s = jnp.einsum('bqhd,bkhd->bhqk', qi, k, preferred_element_type=jnp.float32) * scale
        s = s + ci[:, :, :, None] - cT[:, :, None, :]
        qpos = i * Q_BLOCK + jnp.arange(Q_BLOCK)
        s = jnp.where(kpos[None, :] <= qpos[:, None], s, -jnp.inf)
        pr = jax.nn.softmax(s, axis=-1)
        return jnp.einsum('bhqk,bkhd->bqhd', pr.astype(v.dtype), v)

    o = lax.map(block, (jnp.arange(nb), qb, cqb))
    return jnp.transpose(o, (1, 0, 2, 3, 4)).reshape(B, S, H * dh)

def fox_sample(q, k, v, logf, cache_k, cache_v, cache_logf, page_table):
    DB, T, H, dh = q.shape
    scale = dh ** -0.5
    P = page_table.shape[1] * cache_k.shape[1]
    kp = cache_k[page_table].reshape(DB, P, H, dh).astype(k.dtype)
    vp = cache_v[page_table].reshape(DB, P, H, dh).astype(v.dtype)
    lp = cache_logf[page_table].reshape(DB, P, H).astype(jnp.float32)
    k_all = jnp.concatenate([kp, k], axis=1)
    v_all = jnp.concatenate([vp, v], axis=1)
    c = jnp.cumsum(jnp.concatenate([lp, logf], axis=1), axis=1)
    cT = jnp.transpose(c, (0, 2, 1))
    s = jnp.einsum('bqhd,bkhd->bhqk', q, k_all, preferred_element_type=jnp.float32) * scale
    s = s + cT[:, :, P:, None] - cT[:, :, None, :]
    kpos = jnp.arange(P + T)
    qpos = P + jnp.arange(T)
    s = jnp.where(kpos[None, :] <= qpos[:, None], s, -jnp.inf)
    pr = jax.nn.softmax(s, axis=-1)
    o = jnp.einsum('bhqk,bkhd->bqhd', pr.astype(v.dtype), v_all)
    return o.reshape(DB, T, H * dh)

def swiglu(xn, w_gu, w_down):
    g, u = jnp.split(xn @ w_gu, 2, axis=-1)
    return (jax.nn.silu(g) * u) @ w_down

def setup_inputs(seed: int = 0) -> dict:
    key = jax.random.key(seed)
    ks = jax.random.split(key, 24)
    D, H, F, K = D_MODEL, N_HEADS, D_FF, CONV_WIDTH
    NC, NA = N_CONV_LAYERS, N_ATTN_LAYERS
    n_pages = PAST_LEN // PAGE_SIZE
    n_used = DEC_BATCH * n_pages
    n_phys = n_used + max(1, n_used // 4)
    nrm = jax.random.normal
    f32 = jnp.float32
    page_table = jax.random.permutation(ks[0], n_phys)[:n_used].reshape(DEC_BATCH, n_pages).astype(jnp.int32)
    return {
        "x_prompt": nrm(ks[1], (BATCH, SEQ, D), f32),
        "x_sample": nrm(ks[2], (DEC_BATCH, DEC_SEQ, D), f32),
        "state_conv": 0.5 * nrm(ks[3], (NC, DEC_BATCH, CONV_HIST, D), f32),
        "cache_k": nrm(ks[4], (NA, n_phys, PAGE_SIZE, H, HEAD_DIM), f32),
        "cache_v": nrm(ks[5], (NA, n_phys, PAGE_SIZE, H, HEAD_DIM), f32),
        "cache_logf": jax.nn.log_sigmoid(FORGET_BIAS_MEAN + nrm(ks[6], (NA, n_phys, PAGE_SIZE, H), f32)),
        "page_table": page_table,
        "norm_mix_g": 1.0 + 0.02 * nrm(ks[7], (DEPTH, D), f32),
        "norm_ffn_g": 1.0 + 0.02 * nrm(ks[8], (DEPTH, D), f32),
        "norm_final_g": 1.0 + 0.02 * nrm(ks[9], (D,), f32),
        "conv_w_in": nrm(ks[10], (NC, D, 2 * D), f32) * D ** -0.5,
        "conv_b_in": 0.02 * nrm(ks[11], (NC, 2 * D), f32),
        "conv_w_dw": nrm(ks[12], (NC, K, D), f32) * K ** -0.5,
        "conv_b_dw": 0.02 * nrm(ks[13], (NC, D), f32),
        "conv_ln_g": 1.0 + 0.02 * nrm(ks[14], (NC, D), f32),
        "conv_ln_b": 0.02 * nrm(ks[15], (NC, D), f32),
        "conv_w_out": nrm(ks[16], (NC, D, D), f32) * D ** -0.5,
        "conv_b_out": 0.02 * nrm(ks[17], (NC, D), f32),
        "attn_w_in": nrm(ks[18], (NA, D, 3 * D + H), f32) * D ** -0.5,
        "attn_b_f": FORGET_BIAS_MEAN + nrm(ks[19], (NA, H), f32),
        "attn_w_out": nrm(ks[20], (NA, D, D), f32) * D ** -0.5,
        "ffn_w_gu": nrm(ks[21], (DEPTH, D, 2 * F), f32) * D ** -0.5,
        "ffn_w_down": nrm(ks[22], (DEPTH, F, D), f32) * F ** -0.5,
    }

def reference(x_prompt, x_sample, state_conv, cache_k, cache_v, cache_logf, page_table,
              norm_mix_g, norm_ffn_g, norm_final_g,
              conv_w_in, conv_b_in, conv_w_dw, conv_b_dw, conv_ln_g, conv_ln_b, conv_w_out, conv_b_out,
              attn_w_in, attn_b_f, attn_w_out, ffn_w_gu, ffn_w_down):
    hp, hs = x_prompt, x_sample
    conv_p, conv_s = [], []
    kp_l, vp_l, lp_l, ks_l, vs_l, ls_l = [], [], [], [], [], []
    for i in range(DEPTH):
        j = i // N_MIXERS
        xp_n = rmsnorm(hp, norm_mix_g[i])
        xs_n = rmsnorm(hs, norm_mix_g[i])
        if i % N_MIXERS == 0:
            cw = (conv_w_in[j], conv_b_in[j], conv_w_dw[j], conv_b_dw[j],
                  conv_ln_g[j], conv_ln_b[j], conv_w_out[j], conv_b_out[j])
            zero_hist = jnp.zeros((hp.shape[0], CONV_HIST, hp.shape[2]), hp.dtype)
            mp, new_hp = conv_module(xp_n, zero_hist, *cw)
            ms, new_hs = conv_module(xs_n, state_conv[j], *cw)
            conv_p.append(new_hp)
            conv_s.append(new_hs)
        else:
            q, k, v, lf = fox_proj(xp_n, attn_w_in[j], attn_b_f[j])
            mp = fox_prompt(q, k, v, lf) @ attn_w_out[j]
            kp_l.append(k); vp_l.append(v); lp_l.append(lf)
            q, k, v, lf = fox_proj(xs_n, attn_w_in[j], attn_b_f[j])
            ms = fox_sample(q, k, v, lf, cache_k[j], cache_v[j], cache_logf[j], page_table) @ attn_w_out[j]
            ks_l.append(k); vs_l.append(v); ls_l.append(lf)
        hp = hp + mp
        hs = hs + ms
        hp = hp + swiglu(rmsnorm(hp, norm_ffn_g[i]), ffn_w_gu[i], ffn_w_down[i])
        hs = hs + swiglu(rmsnorm(hs, norm_ffn_g[i]), ffn_w_gu[i], ffn_w_down[i])
    y_prompt = rmsnorm(hp, norm_final_g)
    y_sample = rmsnorm(hs, norm_final_g)
    return (y_prompt, y_sample,
            jnp.stack(conv_p, 0), jnp.stack(conv_s, 0),
            jnp.stack(kp_l, 0), jnp.stack(vp_l, 0), jnp.stack(lp_l, 0),
            jnp.stack(ks_l, 0), jnp.stack(vs_l, 0), jnp.stack(ls_l, 0))


_drawn_inputs = setup_inputs


def setup_inputs(seed=0):
    import zlib

    import numpy as np

    out = dict(_drawn_inputs(seed))
    spreads = {}
    factors = {'norm_ffn_g': 3.063,
     'norm_final_g': 8.007,
     'conv_b_in': 2.744,
     'conv_ln_g': 3.696,
     'conv_ln_b': 3.955,
     'cache_logf': 7.917,
     'conv_b_out': 4.556}
    for name, (base, spread) in spreads.items():
        noise = np.random.default_rng([zlib.crc32(name.encode()), seed]).standard_normal(out[name].shape)
        drawn = base * np.exp(spread * noise) if base else spread * noise
        out[name] = __import__('jax').numpy.asarray(drawn.astype(out[name].dtype))
    for name, factor in factors.items():
        out[name] = (out[name] * factor).astype(out[name].dtype)
    return out
```

```python
from contextlib import ExitStack

import concourse.bass as bass
from concourse import mybir

F32 = mybir.dt.float32
FR = mybir.dt.float32r
I32 = mybir.dt.int32
ALU = mybir.AluOpType
ACT = mybir.ActivationFunctionType
AX = mybir.AxisListType
ds = bass.ds

P = 128
NEG = -1.0e30


def hybrid_step(nc, x_prompt, x_sample, state_conv, cache_k, cache_v, cache_logf, page_table,
                norm_mix_g, norm_ffn_g, norm_final_g,
                conv_w_in, conv_b_in, conv_w_dw, conv_b_dw, conv_ln_g, conv_ln_b, conv_w_out, conv_b_out,
                attn_w_in, attn_b_f, attn_w_out, ffn_w_gu, ffn_w_down,
                y_prompt, y_sample, conv_state_prompt, conv_state_sample,
                k_prompt, v_prompt, logf_prompt, k_sample, v_sample, logf_sample):
    D = x_prompt.shape[2]
    SEQ = x_prompt.shape[1]
    NREQ, TNEW = x_sample.shape[0], x_sample.shape[1]
    NS = NREQ * TNEW
    T = SEQ + NS
    C = D // P
    NB = 3
    BW = T // NB
    NT = SEQ // P
    F = ffn_w_down.shape[1]
    FC = F // P
    KW = conv_w_dw.shape[1]
    HIST = KW - 1
    H = cache_k.shape[3]
    DH = cache_k.shape[4]
    NPG = page_table.shape[1]
    NPHYS = cache_k.shape[1]
    EPS = 1e-6
    SCALE = float(DH) ** -0.5
    HSEG = HIST + TNEW
    ULEN = HIST + SEQ + NREQ * HSEG
    US0 = HIST + SEQ
    LAST = T - P
    assert T == NB * BW and BW <= 512 and FC == 22 and C == 8 and NPG == 8 and H * TNEW == 64 and NREQ == 8

    GROUPS = [6, 6, 5, 5]
    NLAYER = 2

    R_MIX, R_FFN, R_FIN, R_BIN, R_BDW, R_LNG, R_LNB, R_BOUT, R_DW = 0, 2, 4, 5, 7, 8, 9, 10, 11
    NPAR = R_DW + KW

    with ExitStack() as ctx:
        def sem(name):
            return ctx.enter_context(nc.semaphore(name))

        where = {}

        def at(name, shape, dt, offset):
            size = 4
            for n in shape[1:]:
                size *= n
            assert offset % 32 == 0 and offset + size <= 229376, (name, offset, size)
            where[name] = (offset, size)
            return nc.alloc_sbuf_tensor_at(name, shape, dt, offset=offset)

        def after(name, pad=32):
            o, s = where[name]
            return (o + s + pad - 1) // pad * pad

        ident = at("ident", [P, P], F32, 16640)
        ones = at("ones", [P, P], F32, after("ident"))
        upper = at("upper", [P, P], F32, after("ones"))
        below = at("below", [P, P], F32, after("upper"))
        cmask = at("cmask", [P, P], F32, after("below"))
        par = at("par", [P, C, NPAR], F32, after("cmask"))
        epst = at("epst", [P, 1], F32, after("par"))
        zero = at("zero", [P, 1], F32, after("epst"))
        X = at("X", [P, C, T], F32, after("zero"))
        ssq = at("ssq", [P, NB, BW], F32, after("X"))
        rs = at("rs", [P, NB, BW], F32, after("ssq"))
        sq = at("sq", [P, NB, BW], F32, after("rs"))
        tm = at("tm", [P, 3, BW], F32, after("sq"))
        wraw = at("wraw", [P, 2, C * P], F32, after("tm"))
        whi = at("whi", [P, 2, C * P], FR, after("wraw"))
        wlo = at("wlo", [P, 2, C * P], FR, after("whi"))
        xhi = at("xhi", [P, C, T], FR, after("wlo"))
        xlo = at("xlo", [P, C, T], FR, after("xhi"))
        GMAX = max(GROUPS)
        hhi = at("hhi", [P, GMAX, T], FR, after("xlo"))
        hlo = at("hlo", [P, GMAX, T], FR, after("hhi"))
        H0 = where["hhi"][0]
        ht = at("ht", [P, NB, BW], F32, after("hlo"))

        xin = at("xin", [P, NT, D], F32, H0)
        xsin = at("xsin", [NS, D], F32, after("xin"))
        hin = at("hin", [NREQ * HIST // 2, 2, D], F32, after("xsin"))
        prow = at("prow", [NPAR, D], F32, where["xlo"][0])
        ycv = at("ycv", [P, C, T], F32, H0)
        u = at("u", [P, ULEN], F32, after("ycv"))
        uprod = at("uprod", [P, NREQ * TNEW, KW], F32, after("u"))
        yacc = at("yacc", [P, SEQ], F32, after("uprod"))
        ys = at("ys", [P, NS], F32, after("yacc"))
        assert after("ys") <= where["ht"][0]
        hist = at("hist", [P, C, NREQ * HIST], F32, after("ht"))
        wc = at("wc", [P, NPAR], F32, after("hist"))
        utail = at("utail", [P, C, HIST + NS], F32, after("wc"))
        ustate = at("ustate", [HIST + NS, D], F32, where["xlo"][0])

        m01 = at("m01", [NS, NREQ, TNEW], F32, after("utail"))
        madd = at("madd", [NS, NREQ, TNEW], F32, after("m01"))

        Vt = at("Vt", [P, NT, D], F32, H0)
        vnew = at("vnew", [NS, D], F32, where["ssq"][0])
        stg = at("stg", [P, 2, T], F32, after("Vt"))
        ktok = at("ktok", [P, 2, NT, P], F32, after("stg"))
        kns = at("kns", [NS, D], F32, where["tm"][0])
        newqk = at("newqk", [P, 2 * C, NS], F32, after("ktok"))
        qbd = at("qbd", [P, C, NREQ, 2 * TNEW], F32, after("newqk"))
        wfr = at("wfr", [P, C, H], F32, after("qbd"))
        wfh = at("wfh", [P, C, H], FR, after("wfr"))
        wfl = at("wfl", [P, C, H], FR, after("wfh"))
        bf = at("bf", [P, H], F32, after("wfl"))
        fz = at("fz", [P, NT + 1, H], F32, after("bf"))
        fe = at("fe", [P, NT + 1, H], F32, after("fz"))
        Lf = at("Lf", [P, NT + 1, H], F32, after("fe"))
        Lnew = at("Lnew", [NS, H], F32, after("Lf"))
        negc = at("negc", [P, NT, H], F32, after("Lnew"))
        negct = at("negct", [H, SEQ], F32, after("negc"))
        NM = at("NM", [NS, NREQ, H, TNEW], F32, after("negct"))
        ptab = at("ptab", [1, NREQ * NPG], I32, after("NM"))
        nmx = at("nmx", [P, 16], F32, after("ptab"))
        den = at("den", [P, 16], F32, after("nmx"))
        rden = at("rden", [P, 16], F32, after("den"))
        m1 = at("m1", [P, H * TNEW], F32, after("rden"))
        mx = at("mx", [64, 1], F32, after("m1"))
        assert after("mx") <= where["m01"][0], (after("mx"), where["m01"][0])
        lc = at("lc", [P, NPG, NREQ, H], F32, where["sq"][0])
        cb = at("cb", [P, NPG, NREQ, H], F32, where["rs"][0])
        qa = at("qa", [DH + 1, 2, SEQ], F32, where["xhi"][0])
        ka = at("ka", [DH + 1, 2, SEQ], F32, after("qa"))
        pr = at("pr", [P, 2, SEQ], F32, after("ka"))
        pt = at("pt", [P, 2, SEQ], F32, after("pr"))
        on = at("on", [P, NT, P], F32, where["tm"][0])
        OT = at("OT", [P, C, T], F32, where["xlo"][0])
        kr = at("kr", [P, 4, D], F32, where["stg"][0])
        assert after("kr") <= where["newqk"][0]
        vr = at("vr", [P, NPG, D], F32, where["xhi"][0])
        KT = at("KT", [P, 2, C, P], F32, H0)
        S = at("S", [P, NPG, H, TNEW], F32, after("KT"))
        Pm = at("Pm", [P, NPG, H * TNEW], F32, after("S"))
        Sn = at("Sn", [NS, H, TNEW], F32, after("Pm"))
        Pn = at("Pn", [NS, H * TNEW], F32, after("Sn"))
        rd = at("rd", [P, H * TNEW], F32, after("Pn"))
        yn = at("yn", [P, C, T], F32, where["xhi"][0])
        ytok = at("ytok", [P, 2, D], F32, H0)

        q_scr = nc.dram_tensor("q_scr", (D, SEQ), F32).ap()
        k_scr = nc.dram_tensor("k_scr", (D, SEQ), F32).ap()
        c_scr = nc.dram_tensor("c_scr", (H, SEQ), F32).ap()

        PS = ctx.enter_context(nc.psum_tensor("PS", [P, 8, 512], F32))

        s_const = sem("s_const")
        s_par_ld = sem("s_par_ld")
        s_x_ld = [sem(f"s_x_ld{i}") for i in range(3)]
        s_hist_ld = sem("s_hist_ld")
        s_tr0 = sem("s_tr0")
        s_ev0 = sem("s_ev0")
        s_xin = [sem("s_xin0"), sem("s_xin1")]
        w_ld = [sem("w_ld0"), sem("w_ld1")]
        w_hi = sem("w_hi")
        w_lo = sem("w_lo")
        mm = sem("mm")
        ev = [sem("ev0"), sem("ev1")]
        s_xev = [sem("s_xev0"), sem("s_xev1")]
        gate = sem("gate")
        s_sq = sem("s_sq")
        s_ssq = sem("s_ssq")
        s_zero = sem("s_zero")
        n_mm = sem("n_mm")
        n_sqrt = sem("n_sqrt")
        n_rec = sem("n_rec")
        n_tm = sem("n_tm")
        n_hi = sem("n_hi")
        n_lo = sem("n_lo")
        l_mm = sem("l_mm")
        l_d = sem("l_d")
        l_sq = sem("l_sq")
        l_silu = sem("l_silu")
        cv = sem("cv")
        c_done = sem("c_done")
        st_tr = sem("st_tr")
        st_ev = sem("st_ev")
        st_out = sem("st_out")
        h_hi = sem("h_hi")
        out_st = sem("out_st")
        out_st2 = sem("out_st2")

        f_ld = sem("f_ld")
        f_hi = sem("f_hi")
        f_lo = sem("f_lo")
        f_mm = sem("f_mm")
        f_z = sem("f_z")
        f_e = sem("f_e")
        nqk = sem("nqk")
        stg_st = [sem("stg_st0"), sem("stg_st1")]
        kt_tr = sem("kt_tr")
        kt_ev = sem("kt_ev")
        kt_st = [sem("kt_st0"), sem("kt_st1")]
        c_mm = sem("c_mm")
        c_neg = sem("c_neg")
        c_tr = sem("c_tr")
        c_nc = sem("c_nc")
        c_st = sem("c_st")
        lc_ld = sem("lc_ld")
        x_mm = sem("x_mm")
        x_ev = sem("x_ev")
        a_ones = sem("a_ones")
        a_ld = [sem("a_ld0"), sem("a_ld1")]
        a_sc = sem("a_sc")
        a_mk = sem("a_mk")
        a_max = sem("a_max")
        a_exp = sem("a_exp")
        a_tr = sem("a_tr")
        a_pt = sem("a_pt")
        a_pv = sem("a_pv")
        a_rec = sem("a_rec")
        a_on = sem("a_on")
        o_tr = sem("o_tr")
        o_ev = sem("o_ev")
        k_ld = [sem(f"k_ld{i}") for i in range(4)]
        v_ld = sem("v_ld")
        k_tr = sem("k_tr")
        k_ea = sem("k_ea")
        k_ed = sem("k_ed")
        k_sc = sem("k_sc")
        d_s = sem("d_s")
        m_pe = sem("m_pe")
        s_exp = sem("s_exp")
        p_den = sem("p_den")
        p_pv = sem("p_pv")
        d_o = sem("d_o")
        o_hi = sem("o_hi")
        o_lo = sem("o_lo")
        y_n = sem("y_n")
        y_tr = sem("y_tr")
        y_ea = sem("y_ea")
        y_ed = sem("y_ed")
        y_st = [sem("y_st0"), sem("y_st1")]

        block = ctx.enter_context(nc.Block())

        PAIRS_OUT = C // 2
        PAIRS_FFN = sum(GROUPS) + len(GROUPS) * PAIRS_OUT
        Q_CONV_IN = 0
        Q_CONV_OUT = Q_CONV_IN + C
        Q_FFN0 = Q_CONV_OUT + PAIRS_OUT
        Q_ATTN_IN = Q_FFN0 + PAIRS_FFN
        Q_ATTN_OUT = Q_ATTN_IN + 3 * C // 2
        Q_FFN1 = Q_ATTN_OUT + PAIRS_OUT
        Q_END = Q_FFN1 + PAIRS_FFN

        EV = [Q_CONV_IN, Q_CONV_OUT]
        PIECES = NB * C
        NORM_OF_RMS = [0, 2, 3, 4, 5]
        HR = NREQ * HIST // 2
        KCH = KW + TNEW + 6

        def blk(b):
            return slice(b * BW, (b + 1) * BW)

        def seen(s, q, b):
            return q * NB + (b + 1 - NB * EV[s])


        def past(eng, s, value):
            if not isinstance(value, int) or value > 0:
                eng.wait_ge(s, value)

        QK, QV = Q_ATTN_IN + C // 2, Q_ATTN_IN + C
        NTAU = 2 * NT
        NTILES = C * NTAU

        def banks(first, n):
            return PS[:, first:first + 2, :].rearrange("p a f -> p (a f)")[:, 0:n]

        def tok(t):
            return slice(t * P, (t + 1) * P) if t < NT else slice(LAST, T)

        def tmi(b, c):
            return (b * C + c) % 3

        def stages(q0, n, more):
            return (q0, q0 + n) if more else (q0, q0 + n - 1)

        @block.sync
        def _(sp):
            pload = [(R_MIX, 2, norm_mix_g), (R_FFN, 2, norm_ffn_g),
                     (R_FIN, 1, norm_final_g.rearrange("(a d) -> a d", a=1)),
                     (R_BIN, 2, conv_b_in.rearrange("a (b d) -> (a b) d", b=2)), (R_BDW, 1, conv_b_dw),
                     (R_LNG, 1, conv_ln_g), (R_LNB, 1, conv_ln_b), (R_BOUT, 1, conv_b_out),
                     (R_DW, KW, conv_w_dw[0])]

            def load_unit(s, w, row0, kc, col):
                src = w[row0:row0 + kc * P, ds(col, P)].rearrange("(k p) f -> p k f", p=P)
                dst = wraw[:, s, 0:kc * P].rearrange("p (k f) -> p k f", f=P)
                sp.dma_start(dst, src).then_inc(w_ld[s], 16)

            def load_pairs(q0, n, w, row0, kc, cols, first=False):
                if first:
                    for s in range(2):
                        load_unit(s, w, row0, kc, cols(0)[s])
                with sp.Fori(1 if first else 0, n) as i:
                    for s in range(2):
                        sp.wait_ge(w_lo, i * 2 + (2 * q0 + s - 1))
                        load_unit(s, w, row0, kc, cols(i)[s])

            def load_ffn(q, layer):
                f0 = 0
                for g in GROUPS:
                    load_pairs(q, g, ffn_w_gu[layer], 0, C,
                               lambda i: (i * P + f0 * P, i * P + (F + f0 * P)))
                    q += g
                    load_pairs(q, PAIRS_OUT, ffn_w_down[layer], f0 * P, g, two)
                    q += PAIRS_OUT
                    f0 += g

            def two(i):
                return i * (2 * P), i * (2 * P) + P

            load_unit(0, conv_w_in[0], 0, C, 0)
            for r, n, src in pload:
                sp.dma_start(prow[r:r + n, :], src).then_inc(s_par_ld, 16)
            x_tiles = x_prompt[0].rearrange("(t p) d -> p t d", p=P)
            sp.dma_start(xin[:, 0:3, :], x_tiles[:, 0:3, :]).then_inc(s_x_ld[0], 16)
            sp.dma_start(xin[:, 3:6, :], x_tiles[:, 3:6, :]).then_inc(s_x_ld[1], 16)
            sp.dma_start(xin[:, 6:NT, :], x_tiles[:, 6:NT, :]).then_inc(s_x_ld[2], 16)
            sp.dma_start(xsin[:, :], x_sample.rearrange("b t d -> (b t) d")).then_inc(s_x_ld[2], 16)
            sp.dma_start(hin[:, :, :], state_conv[0].rearrange("b t d -> (b t) d").rearrange(
                "(i p) d -> p i d", i=2)).then_inc(s_hist_ld, 16)
            load_unit(1, conv_w_in[0], 0, C, D)
            with sp.Fori(1, C) as i:
                for s in range(2):
                    sp.wait_ge(w_lo, i * 2 + (s - 1))
                    load_unit(s, conv_w_in[0], 0, C, i * P + s * D)
            load_pairs(Q_CONV_OUT, PAIRS_OUT, conv_w_out[0], 0, C, two)
            load_ffn(Q_FFN0, 0)
            load_pairs(Q_ATTN_IN, 2, attn_w_in[0], 0, C, two)
            sp.wait_ge(n_lo, 4 * PIECES)
            sp.dma_start(wfr[:, :, :], attn_w_in[0][:, 3 * D:3 * D + H].rearrange("(k p) h -> p k h", p=P)
                         ).then_inc(f_ld, 16)
            sp.dma_start(bf[:, :], attn_b_f.broadcast_to([P, H])).then_inc(f_ld, 16)
            sp.dma_start(ptab[:, :], page_table.rearrange("(a b) n -> a (b n)", a=1)).then_inc(f_ld, 16)
            load_pairs(Q_ATTN_IN + 2, 2, attn_w_in[0], 0, C,
                       lambda i: (i * (2 * P) + 4 * P, i * (2 * P) + 5 * P))
            sp.wait_ge(f_ld, 48)

            def page(n):
                sp.nop(nofuse=True)
                return sp.value_load(ptab[0:1, ds(n, 1)], min_val=0, max_val=NPHYS - 1)
            with sp.Fori(0, NREQ) as b:
                for j in range(NPG):
                    v = page(b * NPG + j)
                    sp.dma_start(lc[:, j, ds(b, 1), :], cache_logf[0][ds(v, 1)].rearrange("a p h -> p a h")
                                 ).then_inc(lc_ld, 16)
            load_pairs(Q_ATTN_IN + 4, 3 * C // 2 - 4, attn_w_in[0], 0, C,
                       lambda i: (i * (2 * P) + 8 * P, i * (2 * P) + 9 * P))
            load_pairs(Q_ATTN_OUT, 2, attn_w_out[0], 0, C, two)
            sp.wait_ge(mm, Q_ATTN_OUT * 2 * NB)
            for s in range(2):
                sp.wait_ge(stg_st[s], 16 * C)
            sp.wait_ge(c_st, 16)

            def load_head(i, s):
                h = i * 2 + s
                sp.dma_start(qa[0:DH, s, :], q_scr[ds(h * DH, DH), :]).then_inc(a_ld[s], 16)
                sp.dma_start(ka[0:DH, s, :], k_scr[ds(h * DH, DH), :]).then_inc(a_ld[s], 16)
                sp.dma_start(ka[DH:DH + 1, s, :], c_scr[ds(h, 1), :]).then_inc(a_ld[s], 16)
            load_head(0, 0)
            load_head(0, 1)
            with sp.Fori(1, C) as i:
                for s in range(2):
                    sp.wait_ge(a_sc, i * NTAU + (NT * (s + 1) - NTAU))
                    load_head(i, s)

            def load_k(b, j):
                v = page(b * NPG + j)
                sp.dma_start(kr[:, j % 4, :], cache_k[0][ds(v, 1)].rearrange("a p h d -> p (a h d)")
                             ).then_inc(k_ld[j % 4], 16)

            def load_request(b):
                for j in range(NPG):
                    past(sp, k_tr, (b * NPG + (j - 3)) * 2)
                    load_k(b, j)
                if isinstance(b, int):
                    sp.wait_ge(a_pv, NTILES)
                else:
                    sp.wait_ge(p_pv, b)
                for j in range(NPG):
                    v = page(b * NPG + j)
                    sp.dma_start(vr[:, j, :], cache_v[0][ds(v, 1)].rearrange("a p h d -> p (a h d)")
                                 ).then_inc(v_ld, 16)
            for s in range(2):
                sp.wait_ge(kt_st[s], 16 * C // 2)
            load_request(0)
            with sp.Fori(1, NREQ) as b:
                load_request(b)
            load_pairs(Q_ATTN_OUT + 2, 2, attn_w_out[0], 0, C,
                       lambda i: (i * (2 * P) + 4 * P, i * (2 * P) + 5 * P))
            load_ffn(Q_FFN1, 1)
            for t in range(NT + 1):
                sp.wait_ge(y_ea, t + 1)
                sp.wait_ge(y_ed, t + 1)
                if t < NT:
                    sp.dma_start(y_prompt[0, t * P:(t + 1) * P, :], ytok[:, t % 2, :]).then_inc(y_st[t % 2], 16)
                else:
                    sp.dma_start(y_sample.rearrange("b t d -> (b t) d"), ytok[0:NS, t % 2, :]
                                 ).then_inc(y_st[t % 2], 16)
            sp.wait_ge(y_st[0], 16 * (NT // 2 + 1))
            sp.wait_ge(y_st[1], 16 * (NT // 2))

        @block.gpsimd
        def _(pool):
            nc.gpsimd.memset(ident[:, :], 0.0).then_inc(s_const, 1)
            nc.gpsimd.memset(ones[:, :], 1.0).then_inc(s_const, 1)
            nc.gpsimd.memset(epst[:, :], EPS).then_inc(s_const, 1)
            nc.gpsimd.memset(cmask[:, :], 0.0).then_inc(s_const, 1)
            pool.wait_ge(s_const, 4)
            nc.gpsimd.affine_select(out=ident[:, :], in_=ident[:, :], compare_op=ALU.not_equal, fill=1.0,
                                    base=0, pattern=[[-1, P]], channel_multiplier=1).then_inc(s_const, 1)
            nc.gpsimd.affine_select(out=upper[:, :], in_=ones[:, :], compare_op=ALU.is_ge, fill=0.0,
                                    base=0, pattern=[[1, P]], channel_multiplier=-1).then_inc(s_const, 1)
            nc.gpsimd.affine_select(out=below[:, :], in_=ones[:, :], compare_op=ALU.is_gt, fill=0.0,
                                    base=0, pattern=[[-1, P]], channel_multiplier=1).then_inc(s_const, 1)
            nc.gpsimd.affine_select(out=cmask[:, :], in_=cmask[:, :], compare_op=ALU.is_ge, fill=NEG,
                                    base=0, pattern=[[-1, P]], channel_multiplier=1).then_inc(s_const, 1)
            nc.gpsimd.affine_select(out=m01[:, :, :], in_=ones[0:NS, 0:NS].rearrange("p (b t) -> p b t", t=TNEW),
                                    compare_op=ALU.is_ge, fill=0.0, base=0, pattern=[[-TNEW, NREQ], [0, TNEW]],
                                    channel_multiplier=1).then_inc(s_const, 1)
            pool.wait_ge(s_const, 9)
            nc.gpsimd.affine_select(out=m01[:, :, :], in_=m01[:, :, :],
                                    compare_op=ALU.is_ge, fill=0.0, base=0, pattern=[[TNEW, NREQ], [1, TNEW]],
                                    channel_multiplier=-1).then_inc(s_const, 1)
            pool.wait_ge(s_const, 10)
            nc.gpsimd.tensor_scalar(madd[:, :, :], m01[:, :, :], -NEG, NEG, ALU.mult, ALU.add).then_inc(s_const, 1)
            with pool.Fori(0, Q_END) as q:
                for s in range(2):
                    pool.wait_ge(w_hi, q * 2 + (s + 1))
                    nc.gpsimd.tensor_tensor(wlo[:, s, :], wraw[:, s, :], whi[:, s, :].bitcast(F32),
                                            ALU.subtract).then_inc(w_lo, 1)

        @block.tensor
        def _(pe):
            def unit(q, s, kc, hi, lo, before=None, conv=False):
                pe.wait_ge(w_lo, q * 2 + (s + 1))
                for b in range(NB):
                    if conv:
                        if not isinstance(q, int) or q > 0:
                            pe.wait_ge(ev[0], seen(0, q - 1, b))
                    elif not isinstance(q, int) or q > EV[s]:
                        pe.wait_ge(ev[s], seen(s, q - 1, b))
                    out = PS[:, NB * s + b, 0:BW]
                    for k in range(kc):
                        if before:
                            before(b, k)
                        wh, wl = whi[:, s, k * P:(k + 1) * P], wlo[:, s, k * P:(k + 1) * P]
                        nc.tensor.matmul(out, wh, hi[:, k, blk(b)], start=(k == 0), stop=False)
                        nc.tensor.matmul(out, wl, hi[:, k, blk(b)], start=False, stop=False)
                        m = nc.tensor.matmul(out, wh, lo[:, k, blk(b)], start=False, stop=(k == kc - 1))
                    m.then_inc(mm, 1)

            def pairs(q0, n, kc, hi, lo, before=None):
                if before is None:
                    with pe.Fori(q0, q0 + n) as q:
                        unit(q, 0, kc, hi, lo)
                        unit(q, 1, kc, hi, lo)
                    return
                unit(q0, 0, kc, hi, lo, before)
                unit(q0, 1, kc, hi, lo)
                with pe.Fori(q0 + 1, q0 + n) as q:
                    unit(q, 0, kc, hi, lo)
                    unit(q, 1, kc, hi, lo)

            def norm_sums(r):
                for b in range(NB):
                    pe.wait_ge(s_ssq, PIECES * (r + 1) - (NB - 1 - b))
                    if b == 2:
                        pe.wait_ge(n_sqrt, NORM_OF_RMS[r] * NB + 1)
                    nc.tensor.matmul(PS[:, 6 + b % 2, 0:BW], ones[:, :], ssq[:, b, :],
                                     start=True, stop=True).then_inc(n_mm, 1)

            def normed(n):
                def before(b, k):
                    pe.wait_ge(n_lo, (n * NB + b) * C + k + 1)
                return before

            def ffn(q, n_norm):
                for gi, g in enumerate(GROUPS):
                    pairs(q, g, C, xhi, xlo, normed(n_norm) if gi == 0 else None)
                    q += g

                    def hidden(b, k, last=g - 1, done=q - 1):
                        if b == 0 and k == 0:
                            pe.wait_ge(ev[0], seen(0, done - 1, NB - 1))
                        if k == last:
                            pe.wait_ge(ev[0], seen(0, done, b))
                    pairs(q, PAIRS_OUT, g, hhi, hlo, hidden)
                    q += PAIRS_OUT

            pe.wait_ge(s_const, 8)
            for t in range(NT + 1):
                if t % 3 == 0:
                    pe.wait_ge(s_x_ld[t // 3], 32 if t == 6 else 16)
                rows = P if t < NT else NS
                src = xin[:, t, :] if t < NT else xsin[:, :]
                for half in range(2):
                    if t >= 3:
                        pe.wait_ge(s_xev[half], t - 2)
                    for j in range(4):
                        c = 4 * half + j
                        m = nc.tensor.transpose(PS[:, 3 * half + t % 3, j * rows:(j + 1) * rows],
                                                src[:, c * P:(c + 1) * P], ident[0:rows, 0:rows])
                    m.then_inc(s_xin[half], 1)
            pe.wait_ge(s_par_ld, 16 * 9)
            for c in range(C):
                m = nc.tensor.transpose(PS[:, 7, c * NPAR:(c + 1) * NPAR], prow[:, c * P:(c + 1) * P],
                                        ident[0:NPAR, 0:NPAR])
            m.then_inc(s_tr0, 1)
            pe.wait_ge(s_ev0, 1)
            norm_sums(0)
            pe.wait_ge(s_xev[0], NT + 1)
            pe.wait_ge(s_xev[1], NT + 1)
            unit(0, 0, C, xhi, xlo, normed(0), conv=True)
            pe.wait_ge(s_hist_ld, 16)
            pe.wait_ge(n_sqrt, NB)
            for n in range(4):
                i, h = n // 2, n % 2
                if n >= 2:
                    pe.wait_ge(s_ev0, n)
                for j in range(4):
                    c = 4 * h + j
                    m = nc.tensor.transpose(PS[:, 6 + n % 2, j * HR:(j + 1) * HR],
                                            hin[:, i, c * P:(c + 1) * P], ident[0:HR, 0:HR])
                m.then_inc(s_tr0, 1)
            unit(0, 1, C, xhi, xlo, conv=True)
            with pe.Fori(1, C) as q:
                unit(q, 0, C, xhi, xlo, conv=True)
                unit(q, 1, C, xhi, xlo, conv=True)
            pe.wait_ge(c_done, C)
            for c in range(C):
                m = nc.tensor.transpose(PS[0:HIST + NS, 6 + c // 4, (c % 4) * P:(c % 4 + 1) * P],
                                        utail[:, c, :], ident[:, :])
            m.then_inc(st_tr, 1)
            for b in range(NB):
                for c in range(C):
                    m = nc.tensor.matmul(PS[:, b, 0:BW], ones[:, :], ycv[:, c, blk(b)],
                                         start=(c == 0), stop=(c == C - 1))
                m.then_inc(l_mm, 1)
            for b in range(NB):
                for c in range(C):
                    pe.wait_ge(l_sq, b * C + c + 1)
                    nc.tensor.matmul(PS[:, 3 + b, 0:BW], ones[:, :], sq[:, tmi(b, c), :],
                                     start=(c == 0), stop=(c == C - 1)).then_inc(l_mm, 1)
            pe.wait_ge(l_d, PIECES)
            pe.wait_ge(n_sqrt, 2 * NB)
            pairs(Q_CONV_OUT, PAIRS_OUT, C, xhi, xlo, normed(1))
            norm_sums(1)
            ffn(Q_FFN0, 2)
            norm_sums(2)
            pairs(Q_ATTN_IN, C // 2, C, xhi, xlo, normed(3))
            pe.wait_ge(n_sqrt, 4 * NB)
            pe.wait_ge(f_lo, 1)
            for t in range(NT + 1):
                out = PS[:, 6, t * H:(t + 1) * H]
                for k in range(C):
                    nc.tensor.matmul(out, xhi[:, k, tok(t)], wfh[:, k, :], start=(k == 0), stop=False)
                    nc.tensor.matmul(out, xlo[:, k, tok(t)], wfh[:, k, :], start=False, stop=False)
                    m = nc.tensor.matmul(out, xhi[:, k, tok(t)], wfl[:, k, :], start=False, stop=(k == C - 1))
            m.then_inc(f_mm, 1)

            def keys_tr(q, s):
                pe.wait_ge(ev[s], seen(s, q, NB - 1))
                m = (q - QK) * 2 + s
                for half in range(2):
                    past(pe, kt_ev, m * 2 + (half - 1))
                    for j in range(4):
                        tr = nc.tensor.transpose(PS[:, 6 + half, j * P:(j + 1) * P],
                                                 stg[:, s, tok(4 * half + j)], ident[:, :])
                    tr.then_inc(kt_tr, 1)

            unit(QK, 0, C, xhi, xlo)
            unit(QK, 1, C, xhi, xlo)
            pe.wait_ge(f_z, 1)
            keys_tr(QK, 0)
            with pe.Fori(QK + 1, QV) as q:
                unit(q, 0, C, xhi, xlo)
                keys_tr(q - 1, 1)
                unit(q, 1, C, xhi, xlo)
                keys_tr(q, 0)
            keys_tr(QV - 1, 1)
            pe.wait_ge(nqk, 2 * C)
            for half in range(2):
                pe.wait_ge(kt_ev, 2 * C + half - 1)
                for j in range(4):
                    m = nc.tensor.transpose(PS[0:NS, 6 + half, j * P:(j + 1) * P],
                                            newqk[:, C + 4 * half + j, :], ident[:, :])
                m.then_inc(kt_tr, 1)

            def sums(out, tri, rows, later):
                for i in range(NT):
                    others = range(i + 1, NT) if later else range(i)
                    m = nc.tensor.matmul(out(i), tri[:, :], rows(i), start=True, stop=(len(others) == 0))
                    for j in others:
                        m = nc.tensor.matmul(out(i), ones[:, :], rows(j), start=False, stop=(j == others[-1]))
                return m

            pe.wait_ge(f_z, 4)
            pe.wait_ge(kt_ev, 2 * C + 1)
            sums(lambda i: PS[:, 6, i * H:(i + 1) * H], upper, lambda i: Lf[:, i, :], False)
            nc.tensor.matmul(PS[0:NS, 6, NT * H:(NT + 1) * H], m01[:, :, :].rearrange("p b t -> p (b t)"),
                             Lnew[:, :], start=True, stop=True).then_inc(c_mm, 1)

            def v_unit(q, s):
                pe.wait_ge(w_lo, q * 2 + (s + 1))
                for b in range(NB):
                    pe.wait_ge(ev[s], seen(s, q - 1, b))
                    for j, t in enumerate(range(4 * b, min(4 * b + 4, NT + 1))):
                        out = PS[:, NB * s + b, j * P:(j + 1) * P]
                        for k in range(C):
                            wh, wl = whi[:, s, k * P:(k + 1) * P], wlo[:, s, k * P:(k + 1) * P]
                            nc.tensor.matmul(out, xhi[:, k, tok(t)], wh, start=(k == 0), stop=False)
                            nc.tensor.matmul(out, xhi[:, k, tok(t)], wl, start=False, stop=False)
                            m = nc.tensor.matmul(out, xlo[:, k, tok(t)], wh, start=False, stop=(k == C - 1))
                    m.then_inc(mm, 1)

            v_unit(QV, 0)
            v_unit(QV, 1)
            pe.wait_ge(c_neg, 2)
            pe.wait_ge(kt_ev, 2 * C + 2)
            for half in range(2):
                for j in range(4):
                    m = nc.tensor.transpose(PS[0:H, 6 + half, j * P:(j + 1) * P], negc[:, 4 * half + j, :],
                                            ident[:, :])
                m.then_inc(c_tr, 1)
            v_unit(QV + 1, 0)
            v_unit(QV + 1, 1)
            pe.wait_ge(lc_ld, 16 * NREQ * NPG)
            pe.wait_ge(c_nc, 2)
            sums(lambda i: PS[:, 6 + i // 4, (i % 4) * P:(i % 4 + 1) * P], below,
                 lambda i: lc[:, i, :, :].rearrange("p b h -> p (b h)"), True).then_inc(x_mm, 1)
            with pe.Fori(QV + 2, Q_ATTN_OUT) as q:
                v_unit(q, 0)
                v_unit(q, 1)

            for s in range(2):
                pe.wait_ge(ev[s], seen(s, Q_ATTN_OUT - 1, NB - 1))
            pe.wait_ge(x_ev, 2)
            pe.wait_ge(a_ones, 1)

            def probs_tr(base, t):
                pe.wait_ge(a_exp, base + (t + 1))
                past(pe, a_pt, base + t)
                for kb in range(t % NT + 1):
                    m = nc.tensor.transpose(PS[:, 4 + kb // 4, (kb % 4) * P:(kb % 4 + 1) * P],
                                            pr[:, t % 2, kb * P:(kb + 1) * P], ident[:, :])
                m.then_inc(a_tr, 1)

            def values(i, base, t):
                pe.wait_ge(a_pt, base + (t + 1))
                past(pe, a_on, base + (t - 1))
                if t == NTAU - 1:
                    pe.wait_ge(o_ev, i * 2 + 1)
                elif t == 1:
                    past(pe, o_ev, i * 2)
                nb = t % NT + 1
                for kb in range(nb):
                    v = Vt[:, kb, ds(i * P + (t // NT) * DH, DH)]
                    m = nc.tensor.matmul(PS[:, 6 + t % 2, 0:DH],
                                         pt[:, t % 2, kb * P:(kb + 1) * P], v,
                                         start=(kb == 0), stop=(kb == nb - 1))
                m.then_inc(a_pv, 1)

            def outputs_tr(i, half):
                pe.wait_ge(a_on, i * NTAU + (NTAU - 2 + 2 * half))
                if half == 1:
                    pe.wait_ge(o_ev, i * 2 + 1)
                for j in range(4):
                    m = nc.tensor.transpose(PS[:, 7, j * P:(j + 1) * P], on[:, 4 * half + j, :], ident[:, :])
                m.then_inc(o_tr, 1)

            def prompt_pair(i):
                base = i * NTAU
                first = isinstance(i, int)
                for t in range(NTAU):
                    s, qt = t // NT, t % NT
                    if qt == 0:
                        pe.wait_ge(a_ld[s], i * 48 + 48)
                    past(pe, a_exp, base + (t - 1))
                    nk = (qt + 1) * P
                    for k0 in range(0, nk, 512):
                        k1 = min(nk, k0 + 512)
                        m = nc.tensor.matmul(PS[:, 2 * (t % 2) + k0 // 512, 0:k1 - k0],
                                             qa[:, s, qt * P:(qt + 1) * P], ka[:, s, k0:k1],
                                             start=True, stop=True)
                    m.then_inc(a_sc, 1)
                    if t >= 1:
                        probs_tr(base, t - 1)
                    elif not first:
                        probs_tr(base - NTAU, NTAU - 1)
                    if t >= 2:
                        values(i, base, t - 2)
                    elif not first:
                        values(i - 1, base - NTAU, NTAU + t - 2)
                    if not first and t in (0, 2):
                        outputs_tr(i - 1, t // 2)

            prompt_pair(0)
            with pe.Fori(1, C) as i:
                prompt_pair(i)
            probs_tr((C - 1) * NTAU, NTAU - 1)
            values(C - 1, (C - 1) * NTAU, NTAU - 2)
            outputs_tr(C - 1, 0)
            values(C - 1, (C - 1) * NTAU, NTAU - 1)
            outputs_tr(C - 1, 1)
            pe.wait_ge(o_ev, 2 * C)
            pe.wait_ge(nqk, 2 * C + 3)

            def page_tr(b, j):
                n = b * NPG + j
                pe.wait_ge(k_ld[j % 4], b * 32 + (16 * (j // 4) + 16))
                for half in range(2):
                    past(pe, (k_ea, k_ed)[half], n - 1)
                    for c in range(4):
                        m = nc.tensor.transpose(PS[:, 2 * (j % 2) + half, c * P:(c + 1) * P],
                                                kr[:, j % 4, (4 * half + c) * P:(4 * half + c + 1) * P],
                                                ident[:, :])
                    m.then_inc(k_tr, 1)

            def page_scores(b, j):
                n = b * NPG + j
                pe.wait_ge(k_ea, n + 1)
                pe.wait_ge(k_ed, n + 1)
                if j == 0:
                    past(pe, d_s, (b - 1) * 7 + 2)
                for c in range(C):
                    m = nc.tensor.matmul(PS[:, 4, j * 64 + c * 8:j * 64 + c * 8 + 8], KT[:, j % 2, c, :],
                                         qbd[:, c, ds(b, 1), :].rearrange("p a t -> p (a t)"),
                                         start=True, stop=True)
                m.then_inc(k_sc, 1)

            def keys(b):
                page_tr(b, 0)
                for j in range(1, NPG):
                    page_tr(b, j)
                    page_scores(b, j - 1)
                page_scores(b, NPG - 1)
                for c in range(C):
                    m = nc.tensor.matmul(PS[0:NS, 5, c * 8:c * 8 + 8], newqk[:, C + c, :],
                                         qbd[:, c, ds(b, 1), :].rearrange("p a t -> p (a t)"),
                                         start=True, stop=True)
                m.then_inc(k_sc, 1)

            def maxima(b):
                past(pe, d_o, b * 3 - 2)
                pe.wait_ge(d_s, b * 7 + 4)
                pe.nop(nofuse=True)
                nc.tensor.transpose(PS[0:64, 6, 0:P], m1[:, :], ident[:, :]).then_inc(m_pe, 1)
                pe.wait_ge(d_s, b * 7 + 5)
                nc.tensor.matmul(PS[:, 6, P:P + 64], mx[:, 0:1].broadcast_to([64, P]), ident[0:64, 0:64],
                                 start=True, stop=True).then_inc(m_pe, 1)

            def sample_values(b):
                pe.wait_ge(s_exp, b * 2 + 2)
                for k in range(NPG):
                    nc.tensor.matmul(PS[:, 6, 192:256], ones[:, :], Pm[:, k, :], start=(k == 0), stop=False)
                nc.tensor.matmul(PS[:, 6, 192:256], ones[0:NS, :], Pn[:, :], start=False, stop=True
                                 ).then_inc(p_den, 1)
                pe.wait_ge(v_ld, b * (16 * NPG) + 16 * NPG)
                for c in range(C):
                    out = PS[:, 7, c * 8:c * 8 + 8]
                    for k in range(NPG):
                        nc.tensor.matmul(out, vr[:, k, c * P:(c + 1) * P], Pm[:, k, c * 8:c * 8 + 8],
                                         start=(k == 0), stop=False)
                    m = nc.tensor.matmul(out, vnew[:, c * P:(c + 1) * P], Pn[:, c * 8:c * 8 + 8],
                                         start=False, stop=True)
                m.then_inc(p_pv, 1)

            keys(0)
            maxima(0)
            with pe.Fori(1, NREQ) as b:
                keys(b)
                sample_values(b - 1)
                maxima(b)
            sample_values(NREQ - 1)
            pe.wait_ge(d_o, 3 * NREQ)

            def attended(b, k):
                pe.wait_ge(o_lo, b * C + k + 1)
            pairs(Q_ATTN_OUT, PAIRS_OUT, C, xhi, xlo, attended)
            norm_sums(3)
            ffn(Q_FFN1, 4)
            norm_sums(4)
            for t in range(NT + 1):
                n = P if t < NT else NS
                pe.wait_ge(y_n, PIECES - C * (NB - 1 - (t * P + n - 1) // BW))
                for half in range(2):
                    past(pe, (y_ea, y_ed)[half], t - 1)
                    for c in range(4):
                        m = nc.tensor.transpose(PS[0:n, 2 * (t % 2) + half, c * P:(c + 1) * P],
                                                yn[:, 4 * half + c, t * P:t * P + n], ident[:, :])
                    m.then_inc(y_tr, 1)

        @block.scalar
        def _(act):
            def hi_part(q, s):
                act.wait_ge(w_ld[s], q * 16 + 16)
                nc.scalar.activation(whi[:, s, :], wraw[:, s, :], ACT.Copy).then_inc(w_hi, 1)

            def next_hi(q, s):
                act.wait_ge(mm, q * (2 * NB) + (NB * s + NB))
                hi_part(q + 1, s)

            def norm_hi(n, b):
                for c in range(C):
                    act.wait_ge(n_tm, (n * NB + b) * C + c + 1)
                    nc.scalar.activation(xhi[:, c, blk(b)], tm[:, tmi(b, c), :], ACT.Copy).then_inc(n_hi, 1)

            def rms_apply(r):
                n = NORM_OF_RMS[r]
                for b in range(NB):
                    act.wait_ge(n_mm, r * NB + b + 1)
                    nc.scalar.activation(rs[:, b, :], PS[:, 6 + b % 2, 0:BW], ACT.Sqrt,
                                         bias=epst[:, 0:1], scale=1.0 / D).then_inc(n_sqrt, 1)
                    norm_hi(n, b)

            def residual(q0, n, r, more=True):
                def pair(q, prep):
                    for s in range(2):
                        for b in range(NB if r is not None else 0):
                            act.wait_ge(ev[s], seen(s, q, b))
                            act.wait_ge(s_ssq, q * (2 * NB) + (r * PIECES - 2 * NB * q0 + s * NB + b + 1 - NB))
                            act.nop(nofuse=True)
                            nc.scalar.activation(
                                sq[:, b, :], X[:, ds(q * 2 + (s - 2 * q0), 1), blk(b)].rearrange("p a t -> p (a t)"),
                                ACT.Square).then_inc(s_sq, 1)
                        if prep:
                            next_hi(q, s)
                a, e = stages(q0, n, more)
                with act.Fori(a, e) as q:
                    pair(q, True)
                if not more:
                    pair(e, False)

            def ffn(q, r, more=True):
                for gi, g in enumerate(GROUPS):
                    with act.Fori(q, q + g) as i:
                        for b in range(NB):
                            act.wait_ge(mm, i * (2 * NB) + (b + 1))
                            act.wait_ge(ev[0], seen(0, i - 1, b))
                            nc.scalar.activation(ht[:, b, :], PS[:, b, 0:BW], ACT.Silu).then_inc(gate, 1)
                        next_hi(i, 0)
                        for b in range(NB):
                            act.wait_ge(ev[1], seen(1, i, b))
                            act.nop(nofuse=True)
                            nc.scalar.activation(hhi[:, ds(i - q, 1), blk(b)].rearrange("p a t -> p (a t)"),
                                                 ht[:, b, :], ACT.Copy).then_inc(h_hi, 1)
                        next_hi(i, 1)
                    q += g
                    last = gi == len(GROUPS) - 1
                    residual(q, PAIRS_OUT, r if last else None, more or not last)
                    q += PAIRS_OUT

            hi_part(0, 0)
            for t in range(NT + 1):
                act.wait_ge(s_xin[1], t + 1)
                n = P if t < NT else NS
                nc.scalar.activation(X[:, 4:8, t * P:t * P + n],
                                     PS[:, 3 + t % 3, 0:4 * n].rearrange("p (c t) -> p c t", t=n),
                                     ACT.Copy).then_inc(s_xev[1], 1)
            for c in range(C):
                for b in range(NB):
                    if c == 0 and b == 0:
                        act.wait_ge(s_xev[0], NT + 1)
                        act.wait_ge(s_xev[1], NT + 1)
                    if c >= 1:
                        act.wait_ge(s_ssq, (c - 1) * NB + b + 1)
                    nc.scalar.activation(sq[:, b, :], X[:, c, blk(b)], ACT.Square).then_inc(s_sq, 1)
            hi_part(0, 1)
            rms_apply(0)

            act.wait_ge(s_ev0, 1)

            def glu(q):
                next_hi(q, 0)
                for b in range(NB):
                    act.wait_ge(mm, q * (2 * NB) + (NB + b + 1))
                    if not isinstance(q, int) or q > 0:
                        act.wait_ge(ev[0], seen(0, q - 1, b))
                    act.nop(nofuse=True)
                    nc.scalar.activation(ht[:, b, :], PS[:, NB + b, 0:BW], ACT.Sigmoid,
                                         bias=par[:, ds(q, 1), R_BIN + 1:R_BIN + 2].rearrange("p a b -> p (a b)")
                                         ).then_inc(gate, 1)
                next_hi(q, 1)

            glu(0)
            with act.Fori(1, C) as q:
                glu(q)
            act.wait_ge(st_tr, 1)
            nc.scalar.activation(ustate[:, 4 * P:8 * P], PS[0:HIST + NS, 7, :], ACT.Copy).then_inc(st_ev, 1)
            act.wait_ge(st_ev, 2)
            act.dma_start(conv_state_prompt[0, 0], ustate[0:HIST, :]).then_inc(st_out, 16)
            act.dma_start(conv_state_sample[0][:, HIST - TNEW:HIST, :],
                          ustate[HIST:HIST + NS, :]).then_inc(st_out, 16)
            act.dma_start(conv_state_sample[0][:, 0:HIST - TNEW, :],
                          state_conv[0][:, TNEW:HIST, :]).then_inc(out_st2, 16)
            for b in range(NB):
                for c in range(C):
                    i = b * C + c
                    act.wait_ge(l_d, i + 1)
                    if i >= 3:
                        act.wait_ge(l_mm, NB + i - 2)
                    nc.scalar.activation(sq[:, tmi(b, c), :], ycv[:, c, blk(b)], ACT.Square).then_inc(l_sq, 1)
            for b in range(NB):
                act.wait_ge(l_mm, NB + (b + 1) * C)
                nc.scalar.activation(rs[:, b, :], PS[:, 3 + b, 0:BW], ACT.Sqrt,
                                     bias=epst[:, 0:1], scale=1.0 / D).then_inc(n_sqrt, 1)
            for b in range(NB):
                for c in range(C):
                    act.wait_ge(n_tm, (NB + b) * C + c + 1)
                    nc.scalar.activation(tm[:, tmi(b, c), :], tm[:, tmi(b, c), :], ACT.Silu,
                                         bias=par[:, c, R_LNB:R_LNB + 1], scale=par[:, c, R_LNG:R_LNG + 1]
                                         ).then_inc(l_silu, 1)
                    act.wait_ge(l_silu, b * C + c + 1)
                    nc.scalar.activation(xhi[:, c, blk(b)], tm[:, tmi(b, c), :], ACT.Copy).then_inc(n_hi, 1)
            residual(Q_CONV_OUT, PAIRS_OUT, 1, True)
            rms_apply(1)
            ffn(Q_FFN0, 2, True)
            rms_apply(2)

            def store_staged(q, s, scr, q0):
                act.wait_ge(ev[s], seen(s, q, NB - 1))
                act.nop(nofuse=True)
                act.dma_start(scr[ds(q * (2 * P) + (s * P - q0 * 2 * P), P), :], stg[:, s, 0:SEQ]
                              ).then_inc(stg_st[s], 16)

            with act.Fori(Q_ATTN_IN, QK) as q:
                for s in range(2):
                    next_hi(q, s)
                    store_staged(q, s, q_scr, Q_ATTN_IN)
            act.wait_ge(f_ld, 48)
            nc.scalar.activation(wfh[:, :, :], wfr[:, :, :], ACT.Copy).then_inc(f_hi, 1)
            act.wait_ge(f_z, 2)
            nc.scalar.activation(fe[:, :, :], fe[:, :, :], ACT.Exp).then_inc(f_e, 1)
            act.wait_ge(f_e, 1)
            nc.scalar.activation(fe[:, :, :], fe[:, :, :], ACT.Ln, bias=ones[:, 0:1]).then_inc(f_e, 1)
            act.wait_ge(f_z, 4)
            act.dma_start(logf_prompt[0, 0].rearrange("(t p) h -> p t h", p=P), Lf[:, 0:NT, :]).then_inc(out_st, 16)
            act.dma_start(logf_sample[0].rearrange("b t h -> (b t) h"), Lnew[:, :]).then_inc(out_st, 16)

            def keys_out(q, s):
                m = (q - QK) * 2 + s
                past(act, kt_st[s], (q - QK) * 16)
                for half in range(2):
                    act.wait_ge(kt_tr, m * 2 + (half + 1))
                    nc.scalar.activation(ktok[:, s, 4 * half:4 * half + 4, :],
                                         PS[:, 6 + half, :].rearrange("p (t f) -> p t f", f=P), ACT.Copy
                                         ).then_inc(kt_ev, 1)
                act.wait_ge(kt_ev, m * 2 + 2)
                act.nop(nofuse=True)
                act.dma_start(k_prompt[0, 0].rearrange("(t p) h d -> p t (h d)", p=P)[:, :, ds(m * P, P)],
                              ktok[:, s, :, :]).then_inc(kt_st[s], 16)

            next_hi(QK, 0)
            store_staged(QK, 0, k_scr, QK)
            next_hi(QK, 1)
            keys_out(QK, 0)
            store_staged(QK, 1, k_scr, QK)

            def keys_pair(q):
                next_hi(q, 0)
                keys_out(q - 1, 1)
                store_staged(q, 0, k_scr, QK)
                next_hi(q, 1)
                keys_out(q, 0)
                store_staged(q, 1, k_scr, QK)
            keys_pair(QK + 1)
            with act.Fori(QK + 2, QV) as q:
                keys_pair(q)
            keys_out(QV - 1, 1)
            for half in range(2):
                act.wait_ge(kt_tr, 2 * C + half + 1)
                nc.scalar.activation(kns[:, 512 * half:512 * half + 512], PS[0:NS, 6 + half, :], ACT.Copy
                                     ).then_inc(kt_ev, 1)
            act.wait_ge(kt_ev, 2 * C + 2)
            act.dma_start(k_sample[0].rearrange("b t h d -> (b t) (h d)"), kns[:, :]).then_inc(out_st, 16)
            next_hi(QV, 0)
            next_hi(QV, 1)
            act.wait_ge(c_nc, 2)
            act.dma_start(c_scr, negct[:, :]).then_inc(c_st, 16)
            with act.Fori(QV + 1, Q_ATTN_OUT) as q:
                next_hi(q, 0)
                next_hi(q, 1)
            for s in range(2):
                act.wait_ge(ev[s], seen(s, Q_ATTN_OUT - 1, NB - 1))
            act.dma_start(v_prompt[0, 0].rearrange("(t p) h d -> p t (h d)", p=P), Vt[:, :, :]).then_inc(out_st, 16)
            act.dma_start(v_sample[0].rearrange("b t h d -> (b t) (h d)"), vnew[:, :]).then_inc(out_st, 16)

            def probs_out(base, t):
                act.wait_ge(a_tr, base + (t + 1))
                past(act, a_pv, base + (t - 1))
                nk = (t % NT + 1) * P
                nc.scalar.activation(pt[:, t % 2, 0:nk], banks(4, nk), ACT.Copy).then_inc(a_pt, 1)

            def prompt_pair(i):
                base = i * NTAU
                for t in range(NTAU):
                    if t >= 1:
                        probs_out(base, t - 1)
                    elif not isinstance(i, int):
                        probs_out(base - NTAU, NTAU - 1)
                    nk = (t % NT + 1) * P
                    act.wait_ge(a_max, base + (t + 1))
                    past(act, a_tr, base + (t - 1))
                    nc.scalar.activation(pr[:, t % 2, 0:nk], banks(2 * (t % 2), nk), ACT.Exp,
                                         bias=nmx[:, t:t + 1], accum_out=den[:, t:t + 1]).then_inc(a_exp, 1)
            prompt_pair(0)
            with act.Fori(1, C) as i:
                prompt_pair(i)
            probs_out((C - 1) * NTAU, NTAU - 1)

            act.wait_ge(out_st, 16 * 5)

            def sample_step(b):
                for j in range(NPG):
                    n = b * NPG + j
                    act.wait_ge(k_tr, n * 2 + 1)
                    past(act, k_sc, b * 9 + (j - 1 if j >= 2 else j - 2))
                    nc.scalar.activation(KT[:, j % 2, 0:4, :],
                                         PS[:, 2 * (j % 2), :].rearrange("p (c f) -> p c f", f=P), ACT.Copy
                                         ).then_inc(k_ea, 1)
                past(act, p_pv, b)
                act.wait_ge(d_s, b * 7 + 6)
                nc.scalar.activation(Pm[:, :, :], S[:, :, :, :].rearrange("p k h t -> p k (h t)"), ACT.Exp
                                     ).then_inc(s_exp, 1)
                act.wait_ge(d_s, b * 7 + 7)
                nc.scalar.activation(Pn[:, :], Sn[:, :, :].rearrange("p h t -> p (h t)"), ACT.Exp
                                     ).then_inc(s_exp, 1)
            sample_step(0)
            with act.Fori(1, NREQ) as b:
                sample_step(b)
            act.wait_ge(d_o, 3 * NREQ)
            act.wait_ge(o_ev, 2 * C)
            for b in range(NB):
                for c in range(C):
                    nc.scalar.activation(xhi[:, c, blk(b)], OT[:, c, blk(b)], ACT.Copy).then_inc(o_hi, 1)
            residual(Q_ATTN_OUT, PAIRS_OUT, 3)
            rms_apply(3)
            ffn(Q_FFN1, 4, False)
            for b in range(NB):
                act.wait_ge(n_mm, 4 * NB + b + 1)
                nc.scalar.activation(rs[:, b, :], PS[:, 6 + b % 2, 0:BW], ACT.Sqrt,
                                     bias=epst[:, 0:1], scale=1.0 / D).then_inc(n_sqrt, 1)
            for t in range(NT + 1):
                n = P if t < NT else NS
                act.wait_ge(y_tr, 2 * t + 1)
                past(act, y_st[t % 2], 16 * (t // 2))
                nc.scalar.activation(ytok[0:n, t % 2, 0:512], PS[0:n, 2 * (t % 2), :], ACT.Copy).then_inc(y_ea, 1)
            act.wait_ge(st_out, 32)
            act.wait_ge(out_st2, 16)

        @block.vector
        def _(dve):
            def norm_block(n, b, chunk):
                dve.wait_ge(n_sqrt, n * NB + b + 1)
                nc.vector.reciprocal(rs[:, b, :], rs[:, b, :]).then_inc(n_rec, 1)
                dve.wait_ge(n_rec, n * NB + b + 1)

                def lo_part(c):
                    dve.wait_ge(n_hi, (n * NB + b) * C + c + 1)
                    nc.vector.tensor_tensor(xlo[:, c, blk(b)], tm[:, tmi(b, c), :], xhi[:, c, blk(b)].bitcast(F32),
                                            ALU.subtract).then_inc(n_lo, 1)
                for c in range(C):
                    i = (n * NB + b) * C + c
                    if i >= 3:
                        dve.wait_ge(n_lo, i - 2)
                    chunk(b, c).then_inc(n_tm, 1)
                    if c >= 1:
                        lo_part(c - 1)
                lo_part(C - 1)

            def rms_apply(r, row):
                def chunk(b, c):
                    return nc.vector.scalar_tensor_tensor(
                        tm[:, tmi(b, c), :], X[:, c, blk(b)], par[:, c, row:row + 1], rs[:, b, :], ALU.mult, ALU.mult)
                for b in range(NB):
                    norm_block(NORM_OF_RMS[r], b, chunk)

            def clear_sums(r):
                nc.vector.memset(ssq[:, :, :], 0.0).then_inc(s_zero, 1)
                dve.wait_ge(s_zero, r + 1)

            def residual(q0, n, r, bias=False):
                if r is not None:
                    clear_sums(r)
                with dve.Fori(q0, q0 + n) as q:
                    for s in range(2):
                        for b in range(NB):
                            dve.wait_ge(mm, q * (2 * NB) + (s * NB + b + 1))
                            xs = X[:, ds(q * 2 + (s - 2 * q0), 1), blk(b)].rearrange("p a t -> p (a t)")
                            if bias:
                                bc = par[:, ds(q * 2 + (s - 2 * q0), 1), R_BOUT:R_BOUT + 1].rearrange("p a t -> p (a t)")
                                nc.vector.scalar_tensor_tensor(xs, PS[:, NB * s + b, 0:BW], bc, xs,
                                                               ALU.add, ALU.add).then_inc(ev[s], 1)
                            else:
                                nc.vector.tensor_tensor(xs, PS[:, NB * s + b, 0:BW], xs, ALU.add).then_inc(ev[s], 1)
                        for b in range(NB if r is not None else 0):
                            dve.wait_ge(s_sq, q * (2 * NB) + (r * PIECES - 2 * NB * q0 + s * NB + b + 1))
                            nc.vector.tensor_tensor(ssq[:, b, :], ssq[:, b, :], sq[:, b, :], ALU.add
                                                    ).then_inc(s_ssq, 1)

            def ffn(q, r, gated):
                for gi, g in enumerate(GROUPS):
                    with dve.Fori(q, q + g) as i:
                        for b in range(NB):
                            dve.wait_ge(gate, i * NB + ((gated - q) * NB + b + 1))
                            dve.wait_ge(mm, i * (2 * NB) + (NB + b + 1))
                            nc.vector.tensor_tensor(ht[:, b, :], PS[:, NB + b, 0:BW], ht[:, b, :], ALU.mult
                                                    ).then_inc(ev[1], 1)
                        for b in range(NB):
                            dve.wait_ge(h_hi, i * NB + ((gated - C - q) * NB + b + 1))
                            hx = (slice(None), ds(i - q, 1), blk(b))
                            nc.vector.tensor_tensor(hlo[hx].rearrange("p a t -> p (a t)"), ht[:, b, :],
                                                    hhi[hx].rearrange("p a t -> p (a t)").bitcast(F32),
                                                    ALU.subtract).then_inc(ev[0], 1)
                    q += g
                    gated += g
                    residual(q, PAIRS_OUT, r if gi == len(GROUPS) - 1 else None)
                    q += PAIRS_OUT

            nc.vector.memset(ssq[:, :, :], 0.0).then_inc(s_zero, 1)
            for t in range(NT + 1):
                dve.wait_ge(s_xin[0], t + 1)
                n = P if t < NT else NS
                nc.vector.tensor_copy(X[:, 0:4, t * P:t * P + n],
                                      PS[:, t % 3, 0:4 * n].rearrange("p (c t) -> p c t", t=n)).then_inc(s_xev[0], 1)
            dve.wait_ge(s_zero, 1)
            for i in range(PIECES):
                dve.wait_ge(s_sq, i + 1)
                nc.vector.tensor_tensor(ssq[:, i % NB, :], ssq[:, i % NB, :], sq[:, i % NB, :], ALU.add
                                        ).then_inc(s_ssq, 1)
            dve.wait_ge(s_tr0, 1)
            nc.vector.tensor_copy(par[:, :, :], PS[:, 7, 0:C * NPAR].rearrange("p (c r) -> p c r", r=NPAR)
                                  ).then_inc(s_ev0, 1)
            dve.wait_ge(s_ev0, 1)
            rms_apply(0, R_MIX)
            for n in range(4):
                i, h = n // 2, n % 2
                dve.wait_ge(s_tr0, n + 2)
                nc.vector.tensor_copy(hist[:, 4 * h:4 * h + 4, i * HR:(i + 1) * HR],
                                      PS[:, 6 + n % 2, 0:4 * HR].rearrange("p (c t) -> p c t", t=HR)
                                      ).then_inc(s_ev0, 1)
            dve.wait_ge(s_ev0, 5)
            nc.vector.memset(u[:, 0:HIST], 0.0).then_inc(cv, 1)

            us = u[:, US0:ULEN].rearrange("p (b t) -> p b t", t=HSEG)
            up = uprod[:, :, :].rearrange("p (b t) k -> p b t k", t=TNEW)
            with dve.Fori(0, C) as c:
                n = [0]

                def step(ins):
                    n[0] += 1
                    ins.then_inc(cv, 1)

                def stepped(m):
                    dve.wait_ge(cv, c * KCH + (m + 1))

                step(nc.vector.tensor_copy(wc[:, :], par[:, ds(c, 1), :].rearrange("p a r -> p (a r)")))
                step(nc.vector.tensor_copy(us[:, :, 0:HIST], hist[:, ds(c, 1), :].rearrange(
                    "p a (b t) -> p (a b) t", t=HIST)))
                stepped(1)
                for b in range(NB):
                    dve.wait_ge(gate, c * NB + (b + 1))
                    lo, hi = b * BW, min((b + 1) * BW, SEQ)
                    ins = nc.vector.scalar_tensor_tensor(
                        u[:, HIST + lo:HIST + hi], PS[:, b, 0:hi - lo], wc[:, R_BIN:R_BIN + 1], ht[:, b, 0:hi - lo],
                        ALU.add, ALU.mult)
                    if b == NB - 1:
                        step(ins)
                        ins = nc.vector.scalar_tensor_tensor(
                            us[:, :, HIST:HSEG], PS[:, b, hi - lo:BW].rearrange("p (b t) -> p b t", t=TNEW),
                            wc[:, R_BIN:R_BIN + 1], ht[:, b, hi - lo:BW].rearrange("p (b t) -> p b t", t=TNEW),
                            ALU.add, ALU.mult)
                    ins.then_inc(ev[0], 1)
                dve.wait_ge(ev[0], c * NB + NB)
                step(nc.vector.tensor_copy(utail[:, ds(c, 1), 0:HIST].rearrange("p a t -> p (a t)"),
                                           u[:, SEQ:SEQ + HIST]))
                step(nc.vector.tensor_copy(utail[:, ds(c, 1), HIST:HIST + NS].rearrange(
                    "p a (b t) -> p (a b) t", t=TNEW), us[:, :, HIST:HSEG]))
                step(nc.vector.tensor_scalar(yacc[:, :], u[:, 0:SEQ], wc[:, R_DW:R_DW + 1],
                                             wc[:, R_BDW:R_BDW + 1], ALU.mult, ALU.add))
                for k in range(1, KW):
                    have = n[0]
                    if k <= TNEW:
                        t = k - 1
                        step(nc.vector.tensor_tensor(
                            up[:, :, t, :], us[:, :, t:t + KW],
                            wc[:, R_DW:R_DW + KW].rearrange("p (a k) -> p a k", a=1).broadcast_to([P, NREQ, KW]),
                            ALU.mult))
                    if k == TNEW + 2:
                        step(nc.vector.tensor_reduce(ys[:, :], uprod[:, :, :], AX.X, ALU.add))
                    if k == TNEW + 4:
                        step(nc.vector.tensor_scalar(
                            ycv[:, ds(c, 1), SEQ:T].rearrange("p a t -> p (a t)"), ys[:, :],
                            wc[:, R_BDW:R_BDW + 1], None, ALU.add))
                    stepped(have)
                    dst = yacc[:, :] if k < KW - 1 else ycv[:, ds(c, 1), 0:SEQ].rearrange("p a t -> p (a t)")
                    ins = nc.vector.scalar_tensor_tensor(dst, u[:, k:k + SEQ], wc[:, R_DW + k:R_DW + k + 1],
                                                         yacc[:, :], ALU.mult, ALU.add)
                    if k < KW - 1:
                        step(ins)
                    else:
                        ins.then_inc(c_done, 1)
                assert n[0] == KCH, n
                dve.wait_ge(c_done, c + 1)
            dve.wait_ge(st_tr, 1)
            nc.vector.tensor_copy(ustate[:, 0:4 * P], PS[0:HIST + NS, 6, :]).then_inc(st_ev, 1)

            for b in range(NB):
                dve.wait_ge(l_mm, b + 1)
                for c in range(C):
                    nc.vector.scalar_tensor_tensor(ycv[:, c, blk(b)], PS[:, b, 0:BW], -1.0 / D, ycv[:, c, blk(b)],
                                                   ALU.mult, ALU.add).then_inc(l_d, 1)
            dve.wait_ge(st_out, 32)

            def centred(b, c):
                return nc.vector.tensor_tensor(tm[:, tmi(b, c), :], ycv[:, c, blk(b)], rs[:, b, :], ALU.mult)
            for b in range(NB):
                norm_block(1, b, centred)
            residual(Q_CONV_OUT, PAIRS_OUT, 1, bias=True)
            rms_apply(1, R_FFN)
            ffn(Q_FFN0, 2, C)
            rms_apply(2, R_MIX + 1)
            nc.vector.memset(qbd[:, :, :, :], 0.0).then_inc(nqk, 1)

            def qk_pair(q, scale, keys):
                for s in range(2):
                    u = (q - Q_ATTN_IN) * 2 + s
                    past(dve, stg_st[s], (q - Q_ATTN_IN) * 16)
                    if keys:
                        past(dve, kt_tr, ((q - QK) * 2 + (s - 1)) * 2)
                    for b in range(NB):
                        dve.wait_ge(mm, q * (2 * NB) + (s * NB + b + 1))
                        if b == NB - 1:
                            nc.vector.tensor_scalar(
                                newqk[:, ds(u, 1), :].rearrange("p a t -> p (a t)"),
                                PS[:, NB * s + b, BW - NS:BW], scale, None, ALU.mult).then_inc(nqk, 1)
                        nc.vector.tensor_scalar(stg[:, s, blk(b)], PS[:, NB * s + b, 0:BW], scale, None,
                                                ALU.mult).then_inc(ev[s], 1)

            qk_pair(Q_ATTN_IN, SCALE, False)
            with dve.Fori(Q_ATTN_IN + 1, QK) as q:
                qk_pair(q, SCALE, False)
            dve.wait_ge(f_hi, 1)
            nc.vector.tensor_tensor(wfl[:, :, :], wfr[:, :, :], wfh[:, :, :].bitcast(F32), ALU.subtract
                                    ).then_inc(f_lo, 1)
            dve.wait_ge(nqk, C + 1)
            for s in range(2):
                nc.vector.tensor_copy(qbd[64 * s:64 * s + 64, :, :, TNEW * s:TNEW * s + TNEW],
                                      newqk[64 * s:64 * s + 64, 0:C, :].rearrange("p c (b t) -> p c b t", t=TNEW)
                                      ).then_inc(nqk, 1)
            dve.wait_ge(f_mm, 1)
            nc.vector.tensor_tensor(fz[:, :, :], PS[:, 6, 0:(NT + 1) * H].rearrange("p (t h) -> p t h", h=H),
                                    bf[:, :].rearrange("p (a h) -> p a h", a=1).broadcast_to([P, NT + 1, H]),
                                    ALU.add).then_inc(f_z, 1)
            dve.wait_ge(f_z, 1)
            nc.vector.scalar_tensor_tensor(fe[:, :, :], fz[:, :, :], -1.0, fz[:, :, :], ALU.mult, ALU.min
                                           ).then_inc(f_z, 1)
            dve.wait_ge(f_e, 2)
            nc.vector.scalar_tensor_tensor(Lf[:, :, :], fz[:, :, :], 0.0, fe[:, :, :], ALU.min, ALU.subtract
                                           ).then_inc(f_z, 1)
            dve.wait_ge(f_z, 3)
            nc.vector.tensor_copy(Lnew[:, :], Lf[P - NS:P, NT, :]).then_inc(f_z, 1)
            qk_pair(QK, 1.0, False)
            with dve.Fori(QK + 1, QV) as q:
                qk_pair(q, 1.0, True)
            dve.wait_ge(c_mm, 1)
            nc.vector.tensor_scalar(negc[:, :, :], PS[:, 6, 0:NT * H].rearrange("p (t h) -> p t h", h=H),
                                    -1.0, None, ALU.mult).then_inc(c_neg, 1)
            nc.vector.tensor_tensor(
                NM[:, :, :, :],
                madd[:, :, :].rearrange("p b (a t) -> p b a t", a=1).broadcast_to([NS, NREQ, H, TNEW]),
                PS[0:NS, 6, NT * H:(NT + 1) * H].rearrange("p (a h b) -> p a h b", a=1, b=1).broadcast_to(
                    [NS, NREQ, H, TNEW]), ALU.subtract).then_inc(c_neg, 1)

            def v_pair(q):
                for s in range(2):
                    col = q * (2 * P) + (s * P - QV * 2 * P)
                    for b in range(NB):
                        dve.wait_ge(mm, q * (2 * NB) + (s * NB + b + 1))
                        if b < NB - 1:
                            nc.vector.tensor_copy(
                                Vt[:, 4 * b:4 * b + 4, ds(col, P)],
                                PS[:, NB * s + b, :].rearrange("p (t f) -> p t f", f=P)).then_inc(ev[s], 1)
                        else:
                            nc.vector.tensor_copy(vnew[:, ds(col, P)], PS[P - NS:P, NB * s + b, 0:P]
                                                  ).then_inc(ev[s], 1)
            v_pair(QV)
            for half in range(2):
                dve.wait_ge(c_tr, half + 1)
                nc.vector.tensor_copy(negct[:, 512 * half:512 * half + 512], PS[0:H, 6 + half, :]
                                      ).then_inc(c_nc, 1)
            v_pair(QV + 1)
            dve.wait_ge(x_mm, 1)
            for half in range(2):
                nc.vector.tensor_copy(cb[:, 4 * half:4 * half + 4, :, :],
                                      PS[:, 6 + half, :].rearrange("p (k b h) -> p k b h", b=NREQ, h=H)
                                      ).then_inc(x_ev, 1)
            with dve.Fori(QV + 2, Q_ATTN_OUT) as q:
                v_pair(q)

            nc.vector.memset(qa[DH:DH + 1, :, :], 1.0).then_inc(a_ones, 1)
            dve.wait_ge(out_st, 16 * 5)

            def output(i, base, t, first):
                dve.wait_ge(a_pv, base + (t + 1))
                nc.vector.reciprocal(rden[:, t:t + 1], den[:, t:t + 1]).then_inc(a_rec, 1)
                dve.wait_ge(a_rec, base + (t + 1))
                s, qt = t // NT, t % NT
                if s == 0 and not first:
                    dve.wait_ge(o_tr, i * 2 + (qt // 4 - 1))
                nc.vector.tensor_scalar(on[:, qt, s * DH:(s + 1) * DH], PS[:, 6 + t % 2, 0:DH],
                                        rden[:, t:t + 1], None, ALU.mult).then_inc(a_on, 1)

            def outputs_out(i, half):
                dve.wait_ge(o_tr, i * 2 + (half + 1))
                nc.vector.tensor_copy(OT[:, ds(i, 1), 512 * half:512 * half + 512].rearrange("p a t -> p (a t)"),
                                      PS[:, 7, :]).then_inc(o_ev, 1)

            def prompt_pair(i):
                base = i * NTAU
                first = isinstance(i, int)
                for t in range(NTAU):
                    qt = t % NT
                    dve.wait_ge(a_sc, base + (t + 1))
                    diag = banks(2 * (t % 2), (qt + 1) * P)[:, qt * P:(qt + 1) * P]
                    nc.vector.tensor_tensor(diag, diag, cmask[:, :], ALU.add).then_inc(a_mk, 1)
                    dve.wait_ge(a_mk, base + (t + 1))
                    nc.vector.tensor_reduce(nmx[:, t:t + 1], banks(2 * (t % 2), (qt + 1) * P), AX.X, ALU.max,
                                            negate=True).then_inc(a_max, 1)
                    if t >= 2:
                        output(i, base, t - 2, first)
                    elif not first:
                        output(i - 1, base - NTAU, NTAU + t - 2, False)
                    if not first and t in (0, 2):
                        outputs_out(i - 1, t // 2)
            prompt_pair(0)
            with dve.Fori(1, C) as i:
                prompt_pair(i)
            output(C - 1, (C - 1) * NTAU, NTAU - 2, False)
            outputs_out(C - 1, 0)
            output(C - 1, (C - 1) * NTAU, NTAU - 1, False)
            outputs_out(C - 1, 1)

            def cols(ap):
                return ap.rearrange("p (h t) -> p h t", t=TNEW)

            def sample_keys(b):
                for j in range(NPG):
                    n = b * NPG + j
                    dve.wait_ge(k_tr, n * 2 + 2)
                    past(dve, k_sc, b * 9 + (j - 1 if j >= 2 else j - 2))
                    nc.vector.tensor_copy(KT[:, j % 2, 4:8, :],
                                          PS[:, 2 * (j % 2) + 1, :].rearrange("p (c f) -> p c f", f=P)
                                          ).then_inc(k_ed, 1)
                dve.wait_ge(k_sc, b * 9 + 9)
                past(dve, s_exp, b * 2)
                nc.vector.tensor_tensor(
                    S[:, :, :, :], PS[:, 4, :].rearrange("p (k h t) -> p k h t", h=H, t=TNEW),
                    cb[:, :, ds(b, 1), :].rearrange("p k a h -> p k (a h)").rearrange(
                        "p k (h a) -> p k h a", a=1).broadcast_to([P, NPG, H, TNEW]), ALU.add).then_inc(d_s, 1)
                nc.vector.tensor_tensor(Sn[:, :, :], cols(PS[0:NS, 5, 0:64]),
                                        NM[:, ds(b, 1), :, :].rearrange("p a h t -> p (a h) t"), ALU.add
                                        ).then_inc(d_s, 1)
                dve.wait_ge(d_s, b * 7 + 2)
                nc.vector.tensor_reduce(m1[:, :], S[:, :, :, :].rearrange("p k h t -> p (h t) k"), AX.X, ALU.max
                                        ).then_inc(d_s, 1)
                dve.wait_ge(d_s, b * 7 + 3)
                nc.vector.tensor_tensor(m1[0:NS, :], m1[0:NS, :], Sn[:, :, :].rearrange("p h t -> p (h t)"),
                                        ALU.max).then_inc(d_s, 1)

            def sample_shift(b):
                dve.wait_ge(m_pe, b * 2 + 1)
                nc.vector.tensor_reduce(mx[:, 0:1], PS[0:64, 6, 0:P], AX.X, ALU.max).then_inc(d_s, 1)
                dve.wait_ge(m_pe, b * 2 + 2)
                top = PS[:, 6, P:P + 64]
                nc.vector.tensor_tensor(
                    S[:, :, :, :].rearrange("p k h t -> p k (h t)"), S[:, :, :, :].rearrange("p k h t -> p k (h t)"),
                    top.rearrange("p (a c) -> p a c", a=1).broadcast_to([P, NPG, 64]), ALU.subtract
                ).then_inc(d_s, 1)
                nc.vector.tensor_tensor(Sn[:, :, :], Sn[:, :, :], cols(top[0:NS, :]), ALU.subtract
                                        ).then_inc(d_s, 1)

            def sample_out(b):
                dve.wait_ge(p_den, b + 1)
                nc.vector.reciprocal(rd[:, :], PS[:, 6, 192:256]).then_inc(d_o, 1)
                dve.wait_ge(d_o, b * 3 + 1)
                dve.wait_ge(p_pv, b + 1)
                for s in range(2):
                    rows = slice(64 * s, 64 * s + 64)
                    pick = slice(TNEW * s, TNEW * s + TNEW)
                    nc.vector.tensor_tensor(
                        OT[rows, :, ds(b * TNEW + SEQ, TNEW)],
                        PS[rows, 7, 0:64].rearrange("p (c e) -> p c e", e=8)[:, :, pick],
                        rd[rows, :].rearrange("p (c e) -> p c e", e=8)[:, :, pick], ALU.mult).then_inc(d_o, 1)
            sample_keys(0)
            sample_shift(0)
            with dve.Fori(1, NREQ) as b:
                sample_keys(b)
                sample_out(b - 1)
                sample_shift(b)
            sample_out(NREQ - 1)
            for b in range(NB):
                for c in range(C):
                    dve.wait_ge(o_hi, b * C + c + 1)
                    nc.vector.tensor_tensor(xlo[:, c, blk(b)], OT[:, c, blk(b)],
                                            xhi[:, c, blk(b)].bitcast(F32), ALU.subtract).then_inc(o_lo, 1)
            residual(Q_ATTN_OUT, PAIRS_OUT, 3)
            rms_apply(3, R_FFN + 1)
            ffn(Q_FFN1, 4, C + FC)
            for b in range(NB):
                dve.wait_ge(n_sqrt, 5 * NB + b + 1)
                nc.vector.reciprocal(rs[:, b, :], rs[:, b, :]).then_inc(n_rec, 1)
                dve.wait_ge(n_rec, 5 * NB + b + 1)
                for c in range(C):
                    nc.vector.scalar_tensor_tensor(yn[:, c, blk(b)], X[:, c, blk(b)], par[:, c, R_FIN:R_FIN + 1],
                                                   rs[:, b, :], ALU.mult, ALU.mult).then_inc(y_n, 1)
            for t in range(NT + 1):
                n = P if t < NT else NS
                dve.wait_ge(y_tr, 2 * t + 2)
                past(dve, y_st[t % 2], 16 * (t // 2))
                nc.vector.tensor_copy(ytok[0:n, t % 2, 512:1024], PS[0:n, 2 * (t % 2) + 1, :]).then_inc(y_ed, 1)


_NAMES = ["x_prompt", "x_sample", "state_conv", "cache_k", "cache_v", "cache_logf", "page_table",
          "norm_mix_g", "norm_ffn_g", "norm_final_g",
          "conv_w_in", "conv_b_in", "conv_w_dw", "conv_b_dw", "conv_ln_g", "conv_ln_b", "conv_w_out", "conv_b_out",
          "attn_w_in", "attn_b_f", "attn_w_out", "ffn_w_gu", "ffn_w_down"]


def _outputs(inputs):
    _, seq, d = inputs["x_prompt"].shape
    nreq, tnew, _ = inputs["x_sample"].shape
    hist = inputs["conv_w_dw"].shape[1] - 1
    h, dh = inputs["cache_k"].shape[3:]
    return [(1, seq, d), (nreq, tnew, d), (1, 1, hist, d), (1, nreq, hist, d),
            (1, 1, seq, h, dh), (1, 1, seq, h, dh), (1, 1, seq, h),
            (1, nreq, tnew, h, dh), (1, nreq, tnew, h, dh), (1, nreq, tnew, h)]


def kernel(**inputs):
    import numpy as np
    import concourse.bacc as bacc
    from concourse.bass_utils import run_bass_kernel_spmd

    nc = bacc.Bacc("TRN2", target_bir_lowering=False, num_devices=1)
    arrays, args = {}, []
    for name in _NAMES:
        a = np.ascontiguousarray(inputs[name])
        arrays[f"in_{name}"] = a
        args.append(nc.dram_tensor(f"in_{name}", a.shape, mybir.dt.from_np(a.dtype), kind="ExternalInput").ap())
    shapes = _outputs(inputs)
    for i, shape in enumerate(shapes):
        args.append(nc.dram_tensor(f"out_{i}", shape, F32, kind="ExternalOutput").ap())
    hybrid_step(nc, *args)
    got = run_bass_kernel_spmd(nc, [arrays], core_ids=[0]).results[0]
    return tuple(got[f"out_{i}"] for i in range(len(shapes)))
```

```python
from contextlib import ExitStack

import concourse.bass as bass
from concourse import mybir

F32 = mybir.dt.float32
FR = mybir.dt.float32r
I32 = mybir.dt.int32
ALU = mybir.AluOpType
ACT = mybir.ActivationFunctionType
AX = mybir.AxisListType
ds = bass.ds

P = 128
NEG = -1.0e30


def hybrid_step(nc, x_prompt, x_sample, state_conv, cache_k, cache_v, cache_logf, page_table,
                norm_mix_g, norm_ffn_g, norm_final_g,
                conv_w_in, conv_b_in, conv_w_dw, conv_b_dw, conv_ln_g, conv_ln_b, conv_w_out, conv_b_out,
                attn_w_in, attn_b_f, attn_w_out, ffn_w_gu, ffn_w_down,
                y_prompt, y_sample, conv_state_prompt, conv_state_sample,
                k_prompt, v_prompt, logf_prompt, k_sample, v_sample, logf_sample):
    D = x_prompt.shape[2]
    SEQ = x_prompt.shape[1]
    NREQ, TNEW = x_sample.shape[0], x_sample.shape[1]
    NS = NREQ * TNEW
    T = SEQ + NS
    C = D // P
    NB = 3
    BW = T // NB
    NT = SEQ // P
    F = ffn_w_down.shape[1]
    FC = F // P
    KW = conv_w_dw.shape[1]
    HIST = KW - 1
    H = cache_k.shape[3]
    DH = cache_k.shape[4]
    NPG = page_table.shape[1]
    NPHYS = cache_k.shape[1]
    EPS = 1e-6
    SCALE = float(DH) ** -0.5
    HSEG = HIST + TNEW
    ULEN = HIST + SEQ + NREQ * HSEG
    US0 = HIST + SEQ
    LAST = T - P
    assert T == NB * BW and BW <= 512 and FC == 22 and C == 8 and NPG == 8 and H * TNEW == 64 and NREQ == 8

    GROUPS = [6, 6, 5, 5]
    NLAYER = 2

    R_MIX, R_FFN, R_FIN, R_BIN, R_BDW, R_LNG, R_LNB, R_BOUT, R_DW = 0, 2, 4, 5, 7, 8, 9, 10, 11
    NPAR = R_DW + KW

    with ExitStack() as ctx:
        def sem(name):
            return ctx.enter_context(nc.semaphore(name))

        where = {}

        def at(name, shape, dt, offset):
            size = 4
            for n in shape[1:]:
                size *= n
            assert offset % 32 == 0 and offset + size <= 229376, (name, offset, size)
            where[name] = (offset, size)
            return nc.alloc_sbuf_tensor_at(name, shape, dt, offset=offset)

        def after(name, pad=32):
            o, s = where[name]
            return (o + s + pad - 1) // pad * pad

        ident = at("ident", [P, P], F32, 16640)
        ones = at("ones", [P, P], F32, after("ident"))
        upper = at("upper", [P, P], F32, after("ones"))
        below = at("below", [P, P], F32, after("upper"))
        cmask = at("cmask", [P, P], F32, after("below"))
        par = at("par", [P, C, NPAR], F32, after("cmask"))
        epst = at("epst", [P, 1], F32, after("par"))
        zero = at("zero", [P, 1], F32, after("epst"))
        X = at("X", [P, C, T], F32, after("zero"))
        ssq = at("ssq", [P, NB, BW], F32, after("X"))
        rs = at("rs", [P, NB, BW], F32, after("ssq"))
        sq = at("sq", [P, NB, BW], F32, after("rs"))
        tm = at("tm", [P, 3, BW], F32, after("sq"))
        wraw = at("wraw", [P, 2, C * P], F32, after("tm"))
        whi = at("whi", [P, 2, C * P], FR, after("wraw"))
        wlo = at("wlo", [P, 2, C * P], FR, after("whi"))
        xhi = at("xhi", [P, C, T], FR, after("wlo"))
        xlo = at("xlo", [P, C, T], FR, after("xhi"))
        GMAX = max(GROUPS)
        hhi = at("hhi", [P, GMAX, T], FR, after("xlo"))
        hlo = at("hlo", [P, GMAX, T], FR, after("hhi"))
        H0 = where["hhi"][0]
        ht = at("ht", [P, NB, BW], F32, after("hlo"))

        xin = at("xin", [P, NT, D], F32, H0)
        xsin = at("xsin", [NS, D], F32, after("xin"))
        hin = at("hin", [NREQ * HIST // 2, 2, D], F32, after("xsin"))
        prow = at("prow", [NPAR, D], F32, where["xlo"][0])
        ycv = at("ycv", [P, C, T], F32, H0)
        u = at("u", [P, ULEN], F32, after("ycv"))
        uprod = at("uprod", [P, NREQ * TNEW, KW], F32, after("u"))
        yacc = at("yacc", [P, SEQ], F32, after("uprod"))
        ys = at("ys", [P, NS], F32, after("yacc"))
        prods = at("prods", [P, 3, SEQ], F32, where["ssq"][0])
        yp = at("yp", [P, SEQ], F32, where["tm"][0])
        assert after("prods") <= where["tm"][0]
        assert after("ys") <= where["ht"][0]
        hist = at("hist", [P, C, NREQ * HIST], F32, after("ht"))
        wc = at("wc", [P, NPAR], F32, after("hist"))
        utail = at("utail", [P, C, HIST + NS], F32, after("wc"))
        ustate = at("ustate", [HIST + NS, D], F32, where["xlo"][0])

        m01 = at("m01", [NS, NREQ, TNEW], F32, after("utail"))
        isumh = at("isumh", [2 * H, H], F32, where["m01"][0] + 256)
        madd = at("madd", [NS, NREQ, TNEW], F32, after("m01"))

        Vt = at("Vt", [P, NT, D], F32, H0)
        vnew = at("vnew", [NS, D], F32, where["ssq"][0])
        stg = at("stg", [P, 2, T], F32, after("Vt"))
        ktok = at("ktok", [P, 2, NT, P], F32, after("stg"))
        kns = at("kns", [NS, D], F32, where["tm"][0])
        newqk = at("newqk", [P, 3 * C, NS], F32, after("ktok"))
        own = at("own", [P, C, H], F32, after("newqk"))
        isum = at("isum", [P, 64], F32, after("own"))
        NMT = at("NMT", [H * TNEW, NREQ, NS], F32, after("isum"))
        wfr = at("wfr", [P, C, H], F32, after("NMT"))
        bf = at("bf", [P, H], F32, after("wfr"))
        wfs = at("wfs", [P, C, P], FR, where["sq"][0])
        zf = at("zf", [2 * H, T], F32, where["tm"][0])
        fz = at("fz", [P, NT + 1, H], F32, after("bf"))
        fe = at("fe", [P, NT + 1, H], F32, after("fz"))
        Lf = at("Lf", [P, NT + 1, H], F32, after("fe"))
        Lnew = at("Lnew", [NS, H], F32, after("Lf"))
        negc = at("negc", [P, NT, H], F32, after("Lnew"))
        negct = at("negct", [H, SEQ], F32, after("negc"))
        NM = at("NM", [NS, NREQ, H, TNEW], F32, after("negct"))
        ptab = at("ptab", [1, NREQ * NPG], I32, after("NM"))
        nmx = at("nmx", [P, 16], F32, where["wfr"][0])
        den = at("den", [P, 16], F32, after("nmx"))
        rden = at("rden", [P, 16], F32, after("den"))
        smx = at("smx", [H * TNEW, 1], F32, after("rden"))
        sden = at("sden", [H * TNEW, 1], F32, after("smx"))
        srd = at("srd", [P, 1], F32, after("sden"))
        assert after("srd") <= where["bf"][0] and after("ptab") <= where["m01"][0]
        lc = at("lc", [P, NPG, NREQ, H], F32, where["sq"][0])
        cbT = at("cbT", [NREQ * H, NPG * P], F32, where["rs"][0])
        qa = at("qa", [DH + 1, 2, SEQ], F32, where["xhi"][0])
        ka = at("ka", [DH + 1, 2, SEQ], F32, after("qa"))
        pr = at("pr", [P, 2, SEQ], F32, after("ka"))
        pt = at("pt", [P, 2, SEQ], F32, after("pr"))
        on = at("on", [P, NT, P], F32, where["tm"][0])
        OT = at("OT", [P, C, T], F32, where["xlo"][0])
        PAST = NPG * P
        kr = at("kr", [P, 4, D], F32, where["stg"][0])
        assert after("kr") <= where["newqk"][0]
        KTh = at("KTh", [P, 2, C, 2 * P], FR, H0)
        KTl = at("KTl", [P, 2, C, 2 * P], FR, after("KTh"))
        assert after("KTl") <= where["kr"][0]
        vr = at("vr", [P, 2, D], F32, where["xhi"][0])
        Vh = at("Vh", [P, 2, D], FR, after("vr"))
        Vl = at("Vl", [P, 2, D], FR, after("Vh"))
        cbx = at("cbx", [H * TNEW, PAST], F32, after("Vl"))
        qs = at("qs", [P, C, P], FR, after("cbx"))
        assert after("qs") <= where["xlo"][0]
        qx = at("qx", [P, C, H, TNEW], F32, where["NM"][0])
        S = at("S", [H * TNEW, PAST + NS], F32, where["rs"][0])
        Pm = at("Pm", [H * TNEW, PAST + NS], F32, where["sq"][0])
        PTs = at("PTs", [P, NPG, P], FR, where["tm"][0])
        PTn = at("PTn", [NS, P], F32, where["fz"][0])
        ob = at("ob", [P, D], F32, where["negct"][0])
        yn = at("yn", [P, C, T], F32, where["xhi"][0])
        ytok = at("ytok", [P, 2, D], F32, H0)

        q_scr = nc.dram_tensor("q_scr", (D, SEQ), F32).ap()
        k_scr = nc.dram_tensor("k_scr", (D, SEQ), F32).ap()
        c_scr = nc.dram_tensor("c_scr", (H, SEQ), F32).ap()
        cb_scr = nc.dram_tensor("cb_scr", (NREQ * H, NPG * P), F32).ap()

        PS = ctx.enter_context(nc.psum_tensor("PS", [P, 8, 512], F32))

        s_const = sem("s_const")
        s_par_ld = sem("s_par_ld")
        s_x_ld = [sem(f"s_x_ld{i}") for i in range(3)]
        s_hist_ld = sem("s_hist_ld")
        s_tr0 = sem("s_tr0")
        s_ev0 = sem("s_ev0")
        s_xin = [sem("s_xin0"), sem("s_xin1")]
        w_ld = [sem("w_ld0"), sem("w_ld1")]
        w_hi = sem("w_hi")
        w_lo = sem("w_lo")
        mm = sem("mm")
        ev = [sem("ev0"), sem("ev1")]
        s_xev = [sem("s_xev0"), sem("s_xev1")]
        gate = sem("gate")
        s_sq = sem("s_sq")
        s_ssq = sem("s_ssq")
        s_zero = sem("s_zero")
        n_mm = sem("n_mm")
        n_sqrt = sem("n_sqrt")
        n_rec = sem("n_rec")
        n_tm = sem("n_tm")
        n_hi = sem("n_hi")
        n_lo = sem("n_lo")
        l_mm = sem("l_mm")
        l_d = sem("l_d")
        l_sq = sem("l_sq")
        l_silu = sem("l_silu")
        cv = sem("cv")
        a_tap = sem("a_tap")
        p_tap = sem("p_tap")
        c_done = sem("c_done")
        st_tr = sem("st_tr")
        st_ev = sem("st_ev")
        st_out = sem("st_out")
        h_hi = sem("h_hi")
        out_st = sem("out_st")
        out_st2 = sem("out_st2")

        f_ld = sem("f_ld")
        f_hi = sem("f_hi")
        f_lo = sem("f_lo")
        f_mm = sem("f_mm")
        f_z = sem("f_z")
        f_e = sem("f_e")
        nqk = sem("nqk")
        stg_st = [sem("stg_st0"), sem("stg_st1")]
        kt_tr = sem("kt_tr")
        kt_ev = sem("kt_ev")
        kn_tr = sem("kn_tr")
        kn_ev = sem("kn_ev")
        kt_st = [sem("kt_st0"), sem("kt_st1")]
        c_mm = sem("c_mm")
        c_neg = sem("c_neg")
        c_tr = sem("c_tr")
        c_nc = sem("c_nc")
        c_st = sem("c_st")
        lc_ld = sem("lc_ld")
        x_mm = sem("x_mm")
        x_ev = sem("x_ev")
        a_ones = sem("a_ones")
        a_ld = [sem("a_ld0"), sem("a_ld1")]
        a_sc = sem("a_sc")
        a_mk = sem("a_mk")
        a_max = sem("a_max")
        a_exp = sem("a_exp")
        a_tr = sem("a_tr")
        a_pt = sem("a_pt")
        a_pv = sem("a_pv")
        a_rec = sem("a_rec")
        a_on = sem("a_on")
        o_tr = sem("o_tr")
        o_ev = sem("o_ev")
        k_ld = [sem(f"k_ld{i}") for i in range(4)]
        v_ld = [sem("v_ld0"), sem("v_ld1")]
        nm_tr = sem("nm_tr")
        cb_st = sem("cb_st")
        cb_ld = sem("cb_ld")
        d_z = sem("d_z")
        d_q = sem("d_q")
        q_hi = sem("q_hi")
        k_tr = sem("k_tr")
        k_hi = sem("k_hi")
        k_lo = sem("k_lo")
        k_sc = sem("k_sc")
        d_s = sem("d_s")
        s_exp = sem("s_exp")
        pt_tr = sem("pt_tr")
        p_hi = sem("p_hi")
        p_lo = sem("p_lo")
        v_hi = sem("v_hi")
        v_lo = sem("v_lo")
        v_mm = sem("v_mm")
        p_pv = sem("p_pv")
        d_r = sem("d_r")
        d_ob = sem("d_ob")
        o_sel = sem("o_sel")
        d_o = sem("d_o")
        o_hi = sem("o_hi")
        o_lo = sem("o_lo")
        y_n = sem("y_n")
        y_tr = sem("y_tr")
        y_ea = sem("y_ea")
        y_ed = sem("y_ed")
        y_st = [sem("y_st0"), sem("y_st1")]

        block = ctx.enter_context(nc.Block())

        PAIRS_OUT = C // 2
        PAIRS_FFN = sum(GROUPS) + len(GROUPS) * PAIRS_OUT
        Q_CONV_IN = 0
        Q_CONV_OUT = Q_CONV_IN + C
        Q_FFN0 = Q_CONV_OUT + PAIRS_OUT
        Q_ATTN_IN = Q_FFN0 + PAIRS_FFN
        Q_ATTN_OUT = Q_ATTN_IN + 3 * C // 2
        Q_FFN1 = Q_ATTN_OUT + PAIRS_OUT
        Q_END = Q_FFN1 + PAIRS_FFN

        EV = [Q_CONV_IN, Q_CONV_OUT]
        PIECES = NB * C
        NORM_OF_RMS = [0, 2, 3, 4, 5]
        HR = NREQ * HIST // 2
        KP = 12
        KD = KW - KP
        KCH = KD + TNEW + 7

        def blk(b):
            return slice(b * BW, (b + 1) * BW)

        def seen(s, q, b):
            return q * NB + (b + 1 - NB * EV[s])


        def past(eng, s, value):
            if not isinstance(value, int) or value > 0:
                eng.wait_ge(s, value)

        QK, QV = Q_ATTN_IN + C // 2, Q_ATTN_IN + C
        NTAU = 2 * NT
        NTILES = C * NTAU

        def banks(first, n):
            return PS[:, first:first + 2, :].rearrange("p a f -> p (a f)")[:, 0:n]

        def tok(t):
            return slice(t * P, (t + 1) * P) if t < NT else slice(LAST, T)

        def tmi(b, c):
            return (b * C + c) % 3

        def stages(q0, n, more):
            return (q0, q0 + n) if more else (q0, q0 + n - 1)

        @block.sync
        def _(sp):
            pload = [(R_MIX, 2, norm_mix_g), (R_FFN, 2, norm_ffn_g),
                     (R_FIN, 1, norm_final_g.rearrange("(a d) -> a d", a=1)),
                     (R_BIN, 2, conv_b_in.rearrange("a (b d) -> (a b) d", b=2)), (R_BDW, 1, conv_b_dw),
                     (R_LNG, 1, conv_ln_g), (R_LNB, 1, conv_ln_b), (R_BOUT, 1, conv_b_out),
                     (R_DW, KW, conv_w_dw[0])]

            def load_unit(s, w, row0, kc, col):
                src = w[row0:row0 + kc * P, ds(col, P)].rearrange("(k p) f -> p k f", p=P)
                dst = wraw[:, s, 0:kc * P].rearrange("p (k f) -> p k f", f=P)
                sp.dma_start(dst, src).then_inc(w_ld[s], 16)

            def load_pairs(q0, n, w, row0, kc, cols, first=False):
                if first:
                    for s in range(2):
                        load_unit(s, w, row0, kc, cols(0)[s])
                with sp.Fori(1 if first else 0, n) as i:
                    for s in range(2):
                        sp.wait_ge(w_lo, i * 2 + (2 * q0 + s - 1))
                        load_unit(s, w, row0, kc, cols(i)[s])

            def load_ffn(q, layer):
                f0 = 0
                for g in GROUPS:
                    load_pairs(q, g, ffn_w_gu[layer], 0, C,
                               lambda i: (i * P + f0 * P, i * P + (F + f0 * P)))
                    q += g
                    load_pairs(q, PAIRS_OUT, ffn_w_down[layer], f0 * P, g, two)
                    q += PAIRS_OUT
                    f0 += g

            def two(i):
                return i * (2 * P), i * (2 * P) + P

            load_unit(0, conv_w_in[0], 0, C, 0)
            for r, n, src in pload:
                sp.dma_start(prow[r:r + n, :], src).then_inc(s_par_ld, 16)
            x_tiles = x_prompt[0].rearrange("(t p) d -> p t d", p=P)
            sp.dma_start(xin[:, 0:3, :], x_tiles[:, 0:3, :]).then_inc(s_x_ld[0], 16)
            sp.dma_start(xin[:, 3:6, :], x_tiles[:, 3:6, :]).then_inc(s_x_ld[1], 16)
            sp.dma_start(xin[:, 6:NT, :], x_tiles[:, 6:NT, :]).then_inc(s_x_ld[2], 16)
            sp.dma_start(xsin[:, :], x_sample.rearrange("b t d -> (b t) d")).then_inc(s_x_ld[2], 16)
            sp.dma_start(hin[:, :, :], state_conv[0].rearrange("b t d -> (b t) d").rearrange(
                "(i p) d -> p i d", i=2)).then_inc(s_hist_ld, 16)
            load_unit(1, conv_w_in[0], 0, C, D)
            with sp.Fori(1, C) as i:
                for s in range(2):
                    sp.wait_ge(w_lo, i * 2 + (s - 1))
                    load_unit(s, conv_w_in[0], 0, C, i * P + s * D)
            load_pairs(Q_CONV_OUT, PAIRS_OUT, conv_w_out[0], 0, C, two)
            load_ffn(Q_FFN0, 0)
            load_pairs(Q_ATTN_IN, 2, attn_w_in[0], 0, C, two)
            sp.wait_ge(n_lo, 4 * PIECES)
            sp.dma_start(wfr[:, :, :], attn_w_in[0][:, 3 * D:3 * D + H].rearrange("(k p) h -> p k h", p=P)
                         ).then_inc(f_ld, 16)
            sp.dma_start(bf[:, :], attn_b_f.broadcast_to([P, H])).then_inc(f_ld, 16)
            sp.dma_start(ptab[:, :], page_table.rearrange("(a b) n -> a (b n)", a=1)).then_inc(f_ld, 16)
            load_pairs(Q_ATTN_IN + 2, 2, attn_w_in[0], 0, C,
                       lambda i: (i * (2 * P) + 4 * P, i * (2 * P) + 5 * P))
            sp.wait_ge(f_ld, 48)

            def page(n):
                sp.nop(nofuse=True)
                return sp.value_load(ptab[0:1, ds(n, 1)], min_val=0, max_val=NPHYS - 1)
            def load_kv(i):
                for s in range(2):
                    sp.wait_ge(w_lo, i * 2 + (2 * QK + s - 1))
                    load_unit(s, attn_w_in[0], 0, C, i * (2 * P) + (D + s * P))
                if isinstance(i, int):
                    sp.wait_ge(f_mm, NB)
                for j in range(NPG):
                    v = page(i * NPG + j)
                    sp.dma_start(lc[:, j, ds(i, 1), :], cache_logf[0][ds(v, 1)].rearrange("a p h -> p a h")
                                 ).then_inc(lc_ld, 16)
            load_kv(0)
            with sp.Fori(1, C) as i:
                load_kv(i)
            load_pairs(Q_ATTN_OUT, 2, attn_w_out[0], 0, C, two)
            sp.wait_ge(mm, Q_ATTN_OUT * 2 * NB)
            for s in range(2):
                sp.wait_ge(stg_st[s], 16 * C)
            sp.wait_ge(c_st, 16)

            def load_head(i, s):
                h = i * 2 + s
                sp.dma_start(qa[0:DH, s, :], q_scr[ds(h * DH, DH), :]).then_inc(a_ld[s], 16)
                sp.dma_start(ka[0:DH, s, :], k_scr[ds(h * DH, DH), :]).then_inc(a_ld[s], 16)
                sp.dma_start(ka[DH:DH + 1, s, :], c_scr[ds(h, 1), :]).then_inc(a_ld[s], 16)
            load_head(0, 0)
            load_head(0, 1)
            with sp.Fori(1, C) as i:
                for s in range(2):
                    sp.wait_ge(a_sc, i * NTAU + (NT * (s + 1) - NTAU))
                    load_head(i, s)

            def load_k(b, j):
                past(sp, k_tr, b * NPG + (j - 3))
                v = page(b * NPG + j)
                sp.dma_start(kr[:, j % 4, :], cache_k[0][ds(v, 1)].rearrange("a p h d -> p (a h d)")
                             ).then_inc(k_ld[j % 4], 16)

            def load_v(b, j):
                past(sp, v_lo, b * NPG + (j - 1))
                v = page(b * NPG + j)
                sp.dma_start(vr[:, j % 2, :], cache_v[0][ds(v, 1)].rearrange("a p h d -> p (a h d)")
                             ).then_inc(v_ld[j % 2], 16)

            def load_sums(b):
                past(sp, d_s, (b - 1) * 4 + 1)
                sp.dma_start(cbx[:, :],
                             cb_scr[ds(b * H, H), :].rearrange("h (a k) -> h a k", a=1).broadcast_to([H, TNEW, PAST])
                             ).then_inc(cb_ld, 16)

            for s in range(2):
                sp.wait_ge(kt_st[s], 16 * C // 2)
            for j in range(4):
                load_k(0, j)
            sp.wait_ge(a_pv, NTILES)
            sp.wait_ge(cb_st, 16)
            load_sums(0)
            for j in range(4, NPG):
                load_k(0, j)

            def load_step(b):
                for j in range(NPG):
                    load_k(b, j)
                    load_v(b - 1, j)
                    if j == NPG // 2:
                        load_sums(b)
            load_step(1)
            with sp.Fori(2, NREQ) as b:
                load_step(b)
            for j in range(NPG):
                load_v(NREQ - 1, j)
            load_pairs(Q_ATTN_OUT + 2, 2, attn_w_out[0], 0, C,
                       lambda i: (i * (2 * P) + 4 * P, i * (2 * P) + 5 * P))
            load_ffn(Q_FFN1, 1)
            for t in range(NT + 1):
                sp.wait_ge(y_ea, t + 1)
                sp.wait_ge(y_ed, t + 1)
                if t < NT:
                    sp.dma_start(y_prompt[0, t * P:(t + 1) * P, :], ytok[:, t % 2, :]).then_inc(y_st[t % 2], 16)
                else:
                    sp.dma_start(y_sample.rearrange("b t d -> (b t) d"), ytok[0:NS, t % 2, :]
                                 ).then_inc(y_st[t % 2], 16)
            sp.wait_ge(y_st[0], 16 * (NT // 2 + 1))
            sp.wait_ge(y_st[1], 16 * (NT // 2))

        @block.gpsimd
        def _(pool):
            nc.gpsimd.memset(ident[:, :], 0.0).then_inc(s_const, 1)
            nc.gpsimd.memset(ones[:, :], 1.0).then_inc(s_const, 1)
            nc.gpsimd.memset(epst[:, :], EPS).then_inc(s_const, 1)
            nc.gpsimd.memset(cmask[:, :], 0.0).then_inc(s_const, 1)
            pool.wait_ge(s_const, 4)
            nc.gpsimd.affine_select(out=ident[:, :], in_=ident[:, :], compare_op=ALU.not_equal, fill=1.0,
                                    base=0, pattern=[[-1, P]], channel_multiplier=1).then_inc(s_const, 1)
            nc.gpsimd.affine_select(out=upper[:, :], in_=ones[:, :], compare_op=ALU.is_ge, fill=0.0,
                                    base=0, pattern=[[1, P]], channel_multiplier=-1).then_inc(s_const, 1)
            nc.gpsimd.affine_select(out=below[:, :], in_=ones[:, :], compare_op=ALU.is_gt, fill=0.0,
                                    base=0, pattern=[[-1, P]], channel_multiplier=1).then_inc(s_const, 1)
            nc.gpsimd.affine_select(out=cmask[:, :], in_=cmask[:, :], compare_op=ALU.is_ge, fill=NEG,
                                    base=0, pattern=[[-1, P]], channel_multiplier=1).then_inc(s_const, 1)
            nc.gpsimd.affine_select(out=m01[:, :, :], in_=ones[0:NS, 0:NS].rearrange("p (b t) -> p b t", t=TNEW),
                                    compare_op=ALU.is_ge, fill=0.0, base=0, pattern=[[-TNEW, NREQ], [0, TNEW]],
                                    channel_multiplier=1).then_inc(s_const, 1)
            pool.wait_ge(s_const, 9)
            nc.gpsimd.affine_select(out=m01[:, :, :], in_=m01[:, :, :],
                                    compare_op=ALU.is_ge, fill=0.0, base=0, pattern=[[TNEW, NREQ], [1, TNEW]],
                                    channel_multiplier=-1).then_inc(s_const, 1)
            pool.wait_ge(s_const, 10)
            nc.gpsimd.tensor_scalar(madd[:, :, :], m01[:, :, :], -NEG, NEG, ALU.mult, ALU.add).then_inc(s_const, 1)

            nc.gpsimd.memset(isumh[:, :], 0.0).then_inc(s_const, 1)
            for s in range(2):
                pool.wait_ge(s_const, 12 + s)
                nc.gpsimd.affine_select(out=isumh[:, :], in_=isumh[:, :], compare_op=ALU.not_equal, fill=1.0,
                                        base=-H * s, pattern=[[-1, H]], channel_multiplier=1).then_inc(s_const, 1)
            pool.wait_ge(s_const, 14)

            def low_parts(q):
                for s in range(2):
                    pool.wait_ge(w_hi, q * 2 + (s + 1))
                    nc.gpsimd.tensor_tensor(wlo[:, s, :], wraw[:, s, :], whi[:, s, :].bitcast(F32),
                                            ALU.subtract).then_inc(w_lo, 1)
            low_parts(0)
            with pool.Fori(0, C) as c:
                low_parts(c + 1)
                for i in range(1, KP):
                    pool.wait_ge(a_tap, c * KP + (i + 1))
                    if i > 1:
                        pool.wait_ge(p_tap, c * (KP - 1) + (i - 1))
                    pool.nop(nofuse=True)
                    nc.gpsimd.tensor_tensor(yp[:, :], prods[:, 0, :] if i == 1 else yp[:, :], prods[:, i % 3, :],
                                            ALU.add).then_inc(p_tap, 1)
            with pool.Fori(C + 1, QK) as q:
                low_parts(q)
            pool.wait_ge(nqk, 1)
            nc.gpsimd.memset(own[:, :, :], 0.0).then_inc(s_const, 1)
            nc.gpsimd.memset(isum[:, :], 0.0).then_inc(s_const, 1)
            for s in range(2):
                pool.wait_ge(s_const, 16 + 2 * s)
                nc.gpsimd.affine_select(out=own[64 * s:64 * s + 64, :, :], in_=own[64 * s:64 * s + 64, :, :],
                                        compare_op=ALU.not_equal, fill=1.0, base=-s, pattern=[[-2, C], [1, H]],
                                        channel_multiplier=0).then_inc(s_const, 1)
                pool.wait_ge(s_const, 17 + 2 * s)
                nc.gpsimd.affine_select(out=isum[64 * s:64 * s + 64, :], in_=isum[64 * s:64 * s + 64, :],
                                        compare_op=ALU.not_equal, fill=1.0, base=0, pattern=[[-1, 64]],
                                        channel_multiplier=1).then_inc(s_const, 1)
            pool.wait_ge(s_const, 20)
            with pool.Fori(QK, Q_ATTN_OUT + 1) as q:
                low_parts(q)

            def value_lows(b):
                for j in range(NPG):
                    pool.wait_ge(v_hi, b * NPG + (j + 1))
                    past(pool, v_mm, b * NPG + (j - 1))
                    pool.nop(nofuse=True)
                    nc.gpsimd.tensor_tensor(Vl[:, j % 2, :], vr[:, j % 2, :], Vh[:, j % 2, :].bitcast(F32),
                                            ALU.subtract).then_inc(v_lo, 1)
            value_lows(0)
            with pool.Fori(1, NREQ) as b:
                value_lows(b)
            with pool.Fori(Q_ATTN_OUT + 1, Q_END) as q:
                low_parts(q)

        @block.tensor
        def _(pe):
            def unit(q, s, kc, hi, lo, before=None, conv=False):
                pe.wait_ge(w_lo, q * 2 + (s + 1))
                for b in range(NB):
                    if conv:
                        if not isinstance(q, int) or q > 0:
                            pe.wait_ge(ev[0], seen(0, q - 1, b))
                    elif not isinstance(q, int) or q > EV[s]:
                        pe.wait_ge(ev[s], seen(s, q - 1, b))
                    out = PS[:, NB * s + b, 0:BW]
                    for k in range(kc):
                        if before:
                            before(b, k)
                        wh, wl = whi[:, s, k * P:(k + 1) * P], wlo[:, s, k * P:(k + 1) * P]
                        nc.tensor.matmul(out, wh, hi[:, k, blk(b)], start=(k == 0), stop=False)
                        nc.tensor.matmul(out, wl, hi[:, k, blk(b)], start=False, stop=False)
                        m = nc.tensor.matmul(out, wh, lo[:, k, blk(b)], start=False, stop=(k == kc - 1))
                    m.then_inc(mm, 1)

            def pairs(q0, n, kc, hi, lo, before=None):
                if before is None:
                    with pe.Fori(q0, q0 + n) as q:
                        unit(q, 0, kc, hi, lo)
                        unit(q, 1, kc, hi, lo)
                    return
                unit(q0, 0, kc, hi, lo, before)
                unit(q0, 1, kc, hi, lo)
                with pe.Fori(q0 + 1, q0 + n) as q:
                    unit(q, 0, kc, hi, lo)
                    unit(q, 1, kc, hi, lo)

            def norm_sums(r):
                for b in range(NB):
                    pe.wait_ge(s_ssq, PIECES * (r + 1) - (NB - 1 - b))
                    if b == 2:
                        pe.wait_ge(n_sqrt, NORM_OF_RMS[r] * NB + 1)
                    nc.tensor.matmul(PS[:, 6 + b % 2, 0:BW], ones[:, :], ssq[:, b, :],
                                     start=True, stop=True).then_inc(n_mm, 1)

            def normed(n):
                def before(b, k):
                    pe.wait_ge(n_lo, (n * NB + b) * C + k + 1)
                return before

            def ffn(q, n_norm):
                for gi, g in enumerate(GROUPS):
                    pairs(q, g, C, xhi, xlo, normed(n_norm) if gi == 0 else None)
                    q += g

                    def hidden(b, k, last=g - 1, done=q - 1):
                        if b == 0 and k == 0:
                            pe.wait_ge(ev[0], seen(0, done - 1, NB - 1))
                        if k == last:
                            pe.wait_ge(ev[0], seen(0, done, b))
                    pairs(q, PAIRS_OUT, g, hhi, hlo, hidden)
                    q += PAIRS_OUT

            pe.wait_ge(s_const, 8)
            for t in range(NT + 1):
                if t % 3 == 0:
                    pe.wait_ge(s_x_ld[t // 3], 32 if t == 6 else 16)
                rows = P if t < NT else NS
                src = xin[:, t, :] if t < NT else xsin[:, :]
                for half in range(2):
                    if t >= 3:
                        pe.wait_ge(s_xev[half], t - 2)
                    for j in range(4):
                        c = 4 * half + j
                        m = nc.tensor.transpose(PS[:, 3 * half + t % 3, j * rows:(j + 1) * rows],
                                                src[:, c * P:(c + 1) * P], ident[0:rows, 0:rows])
                    m.then_inc(s_xin[half], 1)
            pe.wait_ge(s_par_ld, 16 * 9)
            for c in range(C):
                m = nc.tensor.transpose(PS[:, 7, c * NPAR:(c + 1) * NPAR], prow[:, c * P:(c + 1) * P],
                                        ident[0:NPAR, 0:NPAR])
            m.then_inc(s_tr0, 1)
            pe.wait_ge(s_ev0, 1)
            norm_sums(0)
            pe.wait_ge(s_xev[0], NT + 1)
            pe.wait_ge(s_xev[1], NT + 1)
            unit(0, 0, C, xhi, xlo, normed(0), conv=True)
            pe.wait_ge(s_hist_ld, 16)
            pe.wait_ge(n_sqrt, NB)
            for n in range(4):
                i, h = n // 2, n % 2
                if n >= 2:
                    pe.wait_ge(s_ev0, n)
                for j in range(4):
                    c = 4 * h + j
                    m = nc.tensor.transpose(PS[:, 6 + n % 2, j * HR:(j + 1) * HR],
                                            hin[:, i, c * P:(c + 1) * P], ident[0:HR, 0:HR])
                m.then_inc(s_tr0, 1)
            unit(0, 1, C, xhi, xlo, conv=True)
            with pe.Fori(1, C) as q:
                unit(q, 0, C, xhi, xlo, conv=True)
                unit(q, 1, C, xhi, xlo, conv=True)
            pe.wait_ge(c_done, C)
            for c in range(C):
                m = nc.tensor.transpose(PS[0:HIST + NS, 6 + c // 4, (c % 4) * P:(c % 4 + 1) * P],
                                        utail[:, c, :], ident[:, :])
            m.then_inc(st_tr, 1)
            for b in range(NB):
                for c in range(C):
                    m = nc.tensor.matmul(PS[:, b, 0:BW], ones[:, :], ycv[:, c, blk(b)],
                                         start=(c == 0), stop=(c == C - 1))
                m.then_inc(l_mm, 1)
            for b in range(NB):
                for c in range(C):
                    pe.wait_ge(l_sq, b * C + c + 1)
                    nc.tensor.matmul(PS[:, 3 + b, 0:BW], ones[:, :], sq[:, tmi(b, c), :],
                                     start=(c == 0), stop=(c == C - 1)).then_inc(l_mm, 1)
            pe.wait_ge(l_d, PIECES)
            pe.wait_ge(n_sqrt, 2 * NB)
            pairs(Q_CONV_OUT, PAIRS_OUT, C, xhi, xlo, normed(1))
            norm_sums(1)
            ffn(Q_FFN0, 2)
            norm_sums(2)
            pairs(Q_ATTN_IN, C // 2, C, xhi, xlo, normed(3))
            pe.wait_ge(f_lo, 2)
            for b in range(NB):
                pe.wait_ge(ev[1], seen(1, QK - 1, b))
                for k in range(C):
                    nc.tensor.matmul(PS[:, 3 + b, 0:BW], wfs[:, k, :], xhi[:, k, blk(b)], start=(k == 0), stop=False)
                    m = nc.tensor.matmul(PS[:, 3 + b, 0:BW], wfs[:, k, :], xlo[:, k, blk(b)],
                                         start=False, stop=(k == C - 1))
                m.then_inc(f_mm, 1)
            unit(QK, 0, C, xhi, xlo)
            pe.wait_ge(f_z, NB)
            for t in range(NT + 1):
                m = nc.tensor.matmul(PS[:, 6, t * H:(t + 1) * H], zf[:, tok(t)], isumh[:, :], start=True, stop=True)
            m.then_inc(f_mm, 1)

            def keys_tr(q, s):
                pe.wait_ge(ev[s], seen(s, q, NB - 1))
                m = (q - QK) * 2 + s
                for half in range(2):
                    past(pe, kt_ev, m * 2 + (half - 1))
                    for j in range(4):
                        tr = nc.tensor.transpose(PS[:, 6 + half, j * P:(j + 1) * P],
                                                 stg[:, s, tok(4 * half + j)], ident[:, :])
                    tr.then_inc(kt_tr, 1)

            unit(QK, 1, C, xhi, xlo)
            pe.wait_ge(f_z, NB + 1)
            keys_tr(QK, 0)
            with pe.Fori(QK + 1, QV) as q:
                unit(q, 0, C, xhi, xlo)
                keys_tr(q - 1, 1)
                unit(q, 1, C, xhi, xlo)
                keys_tr(q, 0)
            keys_tr(QV - 1, 1)

            def new_tr(u0, done):
                pe.wait_ge(nqk, u0 + C)
                for half in range(2):
                    pe.wait_ge(kt_ev, done + half - 1)
                    for j in range(4):
                        m = nc.tensor.transpose(PS[0:NS, 6 + half, j * P:(j + 1) * P],
                                                newqk[:, u0 + 4 * half + j, :], ident[:, :])
                    m.then_inc(kn_tr, 1)
            new_tr(C, 2 * C)

            pe.wait_ge(f_z, NB + 4)
            pe.wait_ge(kn_ev, 1)
            for i in range(NT):
                nc.tensor.matmul(PS[:, 6, i * H:(i + 1) * H], upper[:, :], Lf[:, i, :], start=True, stop=(i == 0))
                for j in range(i):
                    nc.tensor.matmul(PS[:, 6, i * H:(i + 1) * H], ones[:, :], Lf[:, j, :], start=False,
                                     stop=(j == i - 1))
            nc.tensor.matmul(PS[0:NS, 6, NT * H:(NT + 1) * H], m01[:, :, :].rearrange("p b t -> p (b t)"),
                             Lnew[:, :], start=True, stop=True).then_inc(c_mm, 1)

            unit(QV, 0, C, xhi, xlo)
            pe.wait_ge(c_neg, 2)
            pe.wait_ge(kn_ev, 2)
            for half in range(2):
                for j in range(4):
                    m = nc.tensor.transpose(PS[0:H, 6 + half, j * P:(j + 1) * P], negc[:, 4 * half + j, :],
                                            ident[:, :])
                m.then_inc(c_tr, 1)
            unit(QV, 1, C, xhi, xlo)
            pe.wait_ge(c_nc, 2)
            keys_tr(QV, 0)
            with pe.Fori(QV + 1, Q_ATTN_OUT) as q:
                unit(q, 0, C, xhi, xlo)
                keys_tr(q - 1, 1)
                unit(q, 1, C, xhi, xlo)
                keys_tr(q, 0)
            keys_tr(Q_ATTN_OUT - 1, 1)
            new_tr(2 * C, 4 * C)
            pe.wait_ge(lc_ld, 16 * NREQ * NPG)
            pe.wait_ge(kn_ev, 4)
            for i in range(NPG):
                out = PS[:, 6 + i // 4, (i % 4) * P:(i % 4 + 1) * P]
                for j in range(i, NPG):
                    m = nc.tensor.matmul(out, lc[:, j, :, :].rearrange("p b h -> p (b h)"),
                                         (below if j == i else ones)[:, :], start=(j == i), stop=(j == NPG - 1))
            m.then_inc(x_mm, 1)

            for s in range(2):
                pe.wait_ge(ev[s], seen(s, Q_ATTN_OUT - 1, NB - 1))
            for b in range(NREQ):
                m = nc.tensor.transpose(PS[0:H * TNEW, 0, b * NS:(b + 1) * NS],
                                        NM[:, b, :, :].rearrange("p h t -> p (h t)"), ident[0:NS, 0:NS])
            m.then_inc(nm_tr, 1)
            pe.wait_ge(x_ev, 3)
            pe.wait_ge(a_ones, 1)

            def probs_tr(base, t):
                pe.wait_ge(a_exp, base + (t + 1))
                past(pe, a_pt, base + t)
                for kb in range(t % NT + 1):
                    m = nc.tensor.transpose(PS[:, 4 + kb // 4, (kb % 4) * P:(kb % 4 + 1) * P],
                                            pr[:, t % 2, kb * P:(kb + 1) * P], ident[:, :])
                m.then_inc(a_tr, 1)

            def values(i, base, t):
                pe.wait_ge(a_pt, base + (t + 1))
                past(pe, a_on, base + (t - 1))
                if t == NTAU - 1:
                    pe.wait_ge(o_ev, i * 2 + 1)
                elif t == 1:
                    past(pe, o_ev, i * 2)
                nb = t % NT + 1
                for kb in range(nb):
                    v = Vt[:, kb, ds(i * P + (t // NT) * DH, DH)]
                    m = nc.tensor.matmul(PS[:, 6 + t % 2, 0:DH],
                                         pt[:, t % 2, kb * P:(kb + 1) * P], v,
                                         start=(kb == 0), stop=(kb == nb - 1))
                m.then_inc(a_pv, 1)

            def outputs_tr(i, half):
                pe.wait_ge(a_on, i * NTAU + (NTAU - 2 + 2 * half))
                if half == 1:
                    pe.wait_ge(o_ev, i * 2 + 1)
                for j in range(4):
                    m = nc.tensor.transpose(PS[:, 7, j * P:(j + 1) * P], on[:, 4 * half + j, :], ident[:, :])
                m.then_inc(o_tr, 1)

            def prompt_pair(i):
                base = i * NTAU
                first = isinstance(i, int)
                for t in range(NTAU):
                    s, qt = t // NT, t % NT
                    if qt == 0:
                        pe.wait_ge(a_ld[s], i * 48 + 48)
                    past(pe, a_exp, base + (t - 1))
                    nk = (qt + 1) * P
                    for k0 in range(0, nk, 512):
                        k1 = min(nk, k0 + 512)
                        m = nc.tensor.matmul(PS[:, 2 * (t % 2) + k0 // 512, 0:k1 - k0],
                                             qa[:, s, qt * P:(qt + 1) * P], ka[:, s, k0:k1],
                                             start=True, stop=True)
                    m.then_inc(a_sc, 1)
                    if t >= 1:
                        probs_tr(base, t - 1)
                    elif not first:
                        probs_tr(base - NTAU, NTAU - 1)
                    if t >= 2:
                        values(i, base, t - 2)
                    elif not first:
                        values(i - 1, base - NTAU, NTAU + t - 2)
                    if not first and t in (0, 2):
                        outputs_tr(i - 1, t // 2)

            prompt_pair(0)
            with pe.Fori(1, C) as i:
                prompt_pair(i)
            probs_tr((C - 1) * NTAU, NTAU - 1)
            values(C - 1, (C - 1) * NTAU, NTAU - 2)
            outputs_tr(C - 1, 0)
            values(C - 1, (C - 1) * NTAU, NTAU - 1)
            outputs_tr(C - 1, 1)
            pe.wait_ge(o_ev, 2 * C)
            pe.wait_ge(s_const, 20)

            def page_tr(b, j):
                n = b * NPG + j
                pe.wait_ge(k_ld[j % 4], b * 32 + (16 * (j // 4) + 16))
                past(pe, k_lo, n - 1)
                if j == 1:
                    past(pe, d_s, b * 4)
                if j == 3:
                    past(pe, p_lo, b * 2)
                for c in range(C):
                    m = nc.tensor.transpose(PS[:, 2 * (j % 2) + c // 4, (c % 4) * P:(c % 4 + 1) * P],
                                            kr[:, j % 4, c * P:(c + 1) * P], ident[:, :])
                m.then_inc(k_tr, 1)

            def scores(b, g):
                pe.wait_ge(k_lo, b * NPG + (2 * g + 2))
                if g == 0:
                    pe.wait_ge(d_q, b * 2 + 2)
                    past(pe, d_s, b * 4)
                out = PS[:, 4 + g // 2, (g % 2) * 2 * P:(g % 2 + 1) * 2 * P]
                for c in range(C):
                    nc.tensor.matmul(out, qs[:, c, :], KTh[:, g % 2, c, :], start=(c == 0), stop=False)
                    m = nc.tensor.matmul(out, qs[:, c, :], KTl[:, g % 2, c, :], start=False, stop=(c == C - 1))
                m.then_inc(k_sc, 1)

            def new_scores(b):
                for c in range(C):
                    m = nc.tensor.matmul(PS[0:H * TNEW, 3, 0:NS], qx[:, c, :, :].rearrange("p h t -> p (h t)"),
                                         newqk[:, C + c, :], start=(c == 0), stop=(c == C - 1))
                m.then_inc(k_sc, 1)

            def exp_tr(b):
                pe.wait_ge(s_exp, b + 1)
                pe.nop(nofuse=True)
                for k in range(NPG):
                    nc.tensor.transpose(PS[:, 2, k * 64:(k + 1) * 64], Pm[:, k * P:(k + 1) * P], ident[0:64, 0:64])
                nc.tensor.transpose(PS[0:NS, 3, 0:64], Pm[:, PAST:PAST + NS], ident[0:64, 0:64]).then_inc(pt_tr, 1)

            def values_page(b, j):
                if j == 0:
                    pe.wait_ge(p_lo, b * 2 + 2)
                    past(pe, d_o, b * 2)
                pe.wait_ge(v_lo, b * NPG + (j + 1))
                for f in range(2):
                    cols = slice(512 * f, 512 * f + 512)
                    nc.tensor.matmul(PS[:, 6 + f, :], PTs[:, j, :], Vh[:, j % 2, cols], start=(j == 0), stop=False)
                    m = nc.tensor.matmul(PS[:, 6 + f, :], PTs[:, j, :], Vl[:, j % 2, cols],
                                         start=False, stop=False)
                m.then_inc(v_mm, 1)
                if j == NPG - 1:
                    for f in range(2):
                        m = nc.tensor.matmul(PS[:, 6 + f, :], PTn[:, :], vnew[:, 512 * f:512 * f + 512],
                                             start=False, stop=True)
                    m.then_inc(p_pv, 1)

            def select(b):
                pe.wait_ge(d_ob, b + 1)
                for c in range(C):
                    m = nc.tensor.matmul(PS[:, 6, c * 8:c * 8 + 8], ob[:, c * P:(c + 1) * P],
                                         isum[:, c * 8:c * 8 + 8], start=True, stop=True)
                m.then_inc(o_sel, 1)

            def request(b, values, selects):
                for j in range(NPG):
                    page_tr(b, j)
                    if j == 0 and selects:
                        select(b - 2)
                    if j >= 2 and j % 2 == 0:
                        scores(b, j // 2 - 1)
                    if j == 2 and values:
                        exp_tr(b - 1)
                    if j >= 2 and values:
                        values_page(b - 1, j - 2)
                scores(b, 3)
                new_scores(b)
                if values:
                    values_page(b - 1, NPG - 2)
                    values_page(b - 1, NPG - 1)
            request(0, False, False)
            request(1, True, False)
            with pe.Fori(2, NREQ) as b:
                request(b, True, True)
            select(NREQ - 2)
            exp_tr(NREQ - 1)
            for j in range(NPG):
                values_page(NREQ - 1, j)
            select(NREQ - 1)
            pe.wait_ge(d_o, 2 * NREQ)

            def attended(b, k):
                pe.wait_ge(o_lo, b * C + k + 1)
            pairs(Q_ATTN_OUT, PAIRS_OUT, C, xhi, xlo, attended)
            norm_sums(3)
            ffn(Q_FFN1, 4)
            norm_sums(4)
            for t in range(NT + 1):
                n = P if t < NT else NS
                pe.wait_ge(y_n, PIECES - C * (NB - 1 - (t * P + n - 1) // BW))
                for half in range(2):
                    past(pe, (y_ea, y_ed)[half], t - 1)
                    for c in range(4):
                        m = nc.tensor.transpose(PS[0:n, 2 * (t % 2) + half, c * P:(c + 1) * P],
                                                yn[:, 4 * half + c, t * P:t * P + n], ident[:, :])
                    m.then_inc(y_tr, 1)

        @block.scalar
        def _(act):
            def hi_part(q, s):
                act.wait_ge(w_ld[s], q * 16 + 16)
                nc.scalar.activation(whi[:, s, :], wraw[:, s, :], ACT.Copy).then_inc(w_hi, 1)

            def next_hi(q, s):
                act.wait_ge(mm, q * (2 * NB) + (NB * s + NB))
                hi_part(q + 1, s)

            def norm_hi(n, b):
                for c in range(C):
                    act.wait_ge(n_tm, (n * NB + b) * C + c + 1)
                    nc.scalar.activation(xhi[:, c, blk(b)], tm[:, tmi(b, c), :], ACT.Copy).then_inc(n_hi, 1)

            def rms_apply(r):
                n = NORM_OF_RMS[r]
                for b in range(NB):
                    act.wait_ge(n_mm, r * NB + b + 1)
                    nc.scalar.activation(rs[:, b, :], PS[:, 6 + b % 2, 0:BW], ACT.Sqrt,
                                         bias=epst[:, 0:1], scale=1.0 / D).then_inc(n_sqrt, 1)
                    norm_hi(n, b)

            def residual(q0, n, r, more=True):
                def pair(q, prep):
                    for s in range(2):
                        for b in range(NB if r is not None else 0):
                            act.wait_ge(ev[s], seen(s, q, b))
                            act.wait_ge(s_ssq, q * (2 * NB) + (r * PIECES - 2 * NB * q0 + s * NB + b + 1 - NB))
                            act.nop(nofuse=True)
                            nc.scalar.activation(
                                sq[:, b, :], X[:, ds(q * 2 + (s - 2 * q0), 1), blk(b)].rearrange("p a t -> p (a t)"),
                                ACT.Square).then_inc(s_sq, 1)
                        if prep:
                            next_hi(q, s)
                a, e = stages(q0, n, more)
                with act.Fori(a, e) as q:
                    pair(q, True)
                if not more:
                    pair(e, False)

            def ffn(q, r, more=True):
                for gi, g in enumerate(GROUPS):
                    with act.Fori(q, q + g) as i:
                        for b in range(NB):
                            act.wait_ge(mm, i * (2 * NB) + (b + 1))
                            act.wait_ge(ev[0], seen(0, i - 1, b))
                            nc.scalar.activation(ht[:, b, :], PS[:, b, 0:BW], ACT.Silu).then_inc(gate, 1)
                        next_hi(i, 0)
                        for b in range(NB):
                            act.wait_ge(ev[1], seen(1, i, b))
                            act.nop(nofuse=True)
                            nc.scalar.activation(hhi[:, ds(i - q, 1), blk(b)].rearrange("p a t -> p (a t)"),
                                                 ht[:, b, :], ACT.Copy).then_inc(h_hi, 1)
                        next_hi(i, 1)
                    q += g
                    last = gi == len(GROUPS) - 1
                    residual(q, PAIRS_OUT, r if last else None, more or not last)
                    q += PAIRS_OUT

            hi_part(0, 0)
            for t in range(NT + 1):
                act.wait_ge(s_xin[1], t + 1)
                n = P if t < NT else NS
                nc.scalar.activation(X[:, 4:8, t * P:t * P + n],
                                     PS[:, 3 + t % 3, 0:4 * n].rearrange("p (c t) -> p c t", t=n),
                                     ACT.Copy).then_inc(s_xev[1], 1)
            for c in range(C):
                for b in range(NB):
                    if c == 0 and b == 0:
                        act.wait_ge(s_xev[0], NT + 1)
                        act.wait_ge(s_xev[1], NT + 1)
                    if c >= 1:
                        act.wait_ge(s_ssq, (c - 1) * NB + b + 1)
                    nc.scalar.activation(sq[:, b, :], X[:, c, blk(b)], ACT.Square).then_inc(s_sq, 1)
            hi_part(0, 1)
            rms_apply(0)

            act.wait_ge(s_ev0, 1)

            def glu(q):
                next_hi(q, 0)
                for b in range(NB):
                    act.wait_ge(mm, q * (2 * NB) + (NB + b + 1))
                    if not isinstance(q, int) or q > 0:
                        act.wait_ge(ev[0], seen(0, q - 1, b))
                    act.nop(nofuse=True)
                    nc.scalar.activation(ht[:, b, :], PS[:, NB + b, 0:BW], ACT.Sigmoid,
                                         bias=par[:, ds(q, 1), R_BIN + 1:R_BIN + 2].rearrange("p a b -> p (a b)")
                                         ).then_inc(gate, 1)
                next_hi(q, 1)
                act.wait_ge(ev[0], seen(0, q, NB - 1))
                for i in range(KP):
                    if i >= 3:
                        act.wait_ge(p_tap, q * (KP - 1) + max(i - 3, 1))
                    else:
                        past(act, p_tap, q * (KP - 1) + (i - 2) if not isinstance(q, int) else 0)
                    act.nop(nofuse=True)
                    k = KD + i
                    nc.scalar.activation(prods[:, i % 3, :], u[:, k:k + SEQ], ACT.Copy,
                                         scale=wc[:, R_DW + k:R_DW + k + 1]).then_inc(a_tap, 1)

            glu(0)
            with act.Fori(1, C) as q:
                glu(q)
            act.wait_ge(st_tr, 1)
            nc.scalar.activation(ustate[:, 4 * P:8 * P], PS[0:HIST + NS, 7, :], ACT.Copy).then_inc(st_ev, 1)
            act.wait_ge(st_ev, 2)
            act.dma_start(conv_state_prompt[0, 0], ustate[0:HIST, :]).then_inc(st_out, 16)
            act.dma_start(conv_state_sample[0][:, HIST - TNEW:HIST, :],
                          ustate[HIST:HIST + NS, :]).then_inc(st_out, 16)
            act.dma_start(conv_state_sample[0][:, 0:HIST - TNEW, :],
                          state_conv[0][:, TNEW:HIST, :]).then_inc(out_st2, 16)
            for b in range(NB):
                for c in range(C):
                    i = b * C + c
                    act.wait_ge(l_d, i + 1)
                    if i >= 3:
                        act.wait_ge(l_mm, NB + i - 2)
                    nc.scalar.activation(sq[:, tmi(b, c), :], ycv[:, c, blk(b)], ACT.Square).then_inc(l_sq, 1)
            for b in range(NB):
                act.wait_ge(l_mm, NB + (b + 1) * C)
                nc.scalar.activation(rs[:, b, :], PS[:, 3 + b, 0:BW], ACT.Sqrt,
                                     bias=epst[:, 0:1], scale=1.0 / D).then_inc(n_sqrt, 1)
            for b in range(NB):
                for c in range(C):
                    act.wait_ge(n_tm, (NB + b) * C + c + 1)
                    nc.scalar.activation(tm[:, tmi(b, c), :], tm[:, tmi(b, c), :], ACT.Silu,
                                         bias=par[:, c, R_LNB:R_LNB + 1], scale=par[:, c, R_LNG:R_LNG + 1]
                                         ).then_inc(l_silu, 1)
                    act.wait_ge(l_silu, b * C + c + 1)
                    nc.scalar.activation(xhi[:, c, blk(b)], tm[:, tmi(b, c), :], ACT.Copy).then_inc(n_hi, 1)
            residual(Q_CONV_OUT, PAIRS_OUT, 1, True)
            rms_apply(1)
            ffn(Q_FFN0, 2, True)
            rms_apply(2)

            def store_staged(q, s, scr, q0):
                act.wait_ge(ev[s], seen(s, q, NB - 1))
                act.nop(nofuse=True)
                act.dma_start(scr[ds(q * (2 * P) + (s * P - q0 * 2 * P), P), :], stg[:, s, 0:SEQ]
                              ).then_inc(stg_st[s], 16)

            with act.Fori(Q_ATTN_IN, QK) as q:
                for s in range(2):
                    next_hi(q, s)
                    store_staged(q, s, q_scr, Q_ATTN_IN)
            act.wait_ge(f_ld, 48)
            nc.scalar.activation(wfs[:, :, 0:H], wfr[:, :, :], ACT.Copy).then_inc(f_hi, 1)
            next_hi(QK, 0)
            store_staged(QK, 0, k_scr, QK)
            act.wait_ge(f_z, NB + 2)
            nc.scalar.activation(fe[:, :, :], fe[:, :, :], ACT.Exp).then_inc(f_e, 1)
            act.wait_ge(f_e, 1)
            nc.scalar.activation(fe[:, :, :], fe[:, :, :], ACT.Ln, bias=ones[:, 0:1]).then_inc(f_e, 1)
            act.wait_ge(f_z, NB + 4)
            act.dma_start(logf_prompt[0, 0].rearrange("(t p) h -> p t h", p=P), Lf[:, 0:NT, :]).then_inc(out_st, 16)
            act.dma_start(logf_sample[0].rearrange("b t h -> (b t) h"), Lnew[:, :]).then_inc(out_st, 16)

            def keys_out(q, s):
                m = (q - QK) * 2 + s
                past(act, kt_st[s], (q - QK) * 16)
                for half in range(2):
                    act.wait_ge(kt_tr, m * 2 + (half + 1))
                    nc.scalar.activation(ktok[:, s, 4 * half:4 * half + 4, :],
                                         PS[:, 6 + half, :].rearrange("p (t f) -> p t f", f=P), ACT.Copy
                                         ).then_inc(kt_ev, 1)
                act.wait_ge(kt_ev, m * 2 + 2)
                act.nop(nofuse=True)
                act.dma_start(k_prompt[0, 0].rearrange("(t p) h d -> p t (h d)", p=P)[:, :, ds(m * P, P)],
                              ktok[:, s, :, :]).then_inc(kt_st[s], 16)

            next_hi(QK, 1)
            keys_out(QK, 0)
            store_staged(QK, 1, k_scr, QK)

            def keys_pair(q):
                next_hi(q, 0)
                keys_out(q - 1, 1)
                store_staged(q, 0, k_scr, QK)
                next_hi(q, 1)
                keys_out(q, 0)
                store_staged(q, 1, k_scr, QK)
            keys_pair(QK + 1)
            with act.Fori(QK + 2, QV) as q:
                keys_pair(q)
            keys_out(QV - 1, 1)

            def new_out(dst, n):
                for half in range(2):
                    act.wait_ge(kn_tr, n + half + 1)
                    nc.scalar.activation(dst[:, 512 * half:512 * half + 512], PS[0:NS, 6 + half, :], ACT.Copy
                                         ).then_inc(kn_ev, 1)
                act.wait_ge(kn_ev, n + 2)
            new_out(kns, 0)
            act.dma_start(k_sample[0].rearrange("b t h d -> (b t) (h d)"), kns[:, :]).then_inc(out_st, 16)

            def values_out(q, s):
                m = (q - QK) * 2 + s
                for half in range(2):
                    act.wait_ge(kt_tr, m * 2 + (half + 1))
                    act.nop(nofuse=True)
                    nc.scalar.activation(Vt[:, 4 * half:4 * half + 4, ds(m * P - D, P)],
                                         PS[:, 6 + half, :].rearrange("p (t f) -> p t f", f=P), ACT.Copy
                                         ).then_inc(kt_ev, 1)
            next_hi(QV, 0)
            next_hi(QV, 1)
            act.wait_ge(c_nc, 2)
            act.dma_start(c_scr, negct[:, :]).then_inc(c_st, 16)
            values_out(QV, 0)
            with act.Fori(QV + 1, Q_ATTN_OUT) as q:
                next_hi(q, 0)
                values_out(q - 1, 1)
                next_hi(q, 1)
                values_out(q, 0)
            values_out(Q_ATTN_OUT - 1, 1)
            new_out(vnew, 2)
            act.wait_ge(kt_ev, 4 * C)
            act.wait_ge(x_ev, 2)
            act.dma_start(cb_scr, cbT[:, :]).then_inc(cb_st, 16)
            act.dma_start(v_prompt[0, 0].rearrange("(t p) h d -> p t (h d)", p=P), Vt[:, :, :]).then_inc(out_st, 16)
            act.dma_start(v_sample[0].rearrange("b t h d -> (b t) (h d)"), vnew[:, :]).then_inc(out_st, 16)

            def probs_out(base, t):
                act.wait_ge(a_tr, base + (t + 1))
                past(act, a_pv, base + (t - 1))
                nk = (t % NT + 1) * P
                nc.scalar.activation(pt[:, t % 2, 0:nk], banks(4, nk), ACT.Copy).then_inc(a_pt, 1)

            def prompt_pair(i):
                base = i * NTAU
                for t in range(NTAU):
                    if t >= 1:
                        probs_out(base, t - 1)
                    elif not isinstance(i, int):
                        probs_out(base - NTAU, NTAU - 1)
                    nk = (t % NT + 1) * P
                    act.wait_ge(a_max, base + (t + 1))
                    past(act, a_tr, base + (t - 1))
                    nc.scalar.activation(pr[:, t % 2, 0:nk], banks(2 * (t % 2), nk), ACT.Exp,
                                         bias=nmx[:, t:t + 1], accum_out=den[:, t:t + 1]).then_inc(a_exp, 1)
            prompt_pair(0)
            with act.Fori(1, C) as i:
                prompt_pair(i)
            probs_out((C - 1) * NTAU, NTAU - 1)

            act.wait_ge(out_st, 16 * 5)

            def key_hi(b, j):
                act.wait_ge(k_tr, b * NPG + (j + 1))
                g = j // 2
                past(act, k_sc, b * 5 + (g - 1 if g >= 2 else g - 2))
                nc.scalar.activation(KTh[:, g % 2, :, (j % 2) * P:(j % 2 + 1) * P],
                                     banks(2 * (j % 2), D).rearrange("p (c f) -> p c f", f=P), ACT.Copy
                                     ).then_inc(k_hi, 1)

            def value_hi(b, j):
                act.wait_ge(v_ld[j % 2], b * (8 * NPG) + (16 * (j // 2) + 16))
                past(act, v_mm, b * NPG + (j - 1))
                nc.scalar.activation(Vh[:, j % 2, :], vr[:, j % 2, :], ACT.Copy).then_inc(v_hi, 1)

            def probs_hi(b):
                act.wait_ge(pt_tr, b + 1)
                past(act, p_pv, b)
                nc.scalar.activation(PTs[:, :, 0:64], PS[:, 2, :].rearrange("p (k c) -> p k c", c=64), ACT.Copy
                                     ).then_inc(p_hi, 1)

            def request(b, values):
                act.wait_ge(d_q, b * 2 + 1)
                nc.scalar.activation(qs[:, :, 0:64], qx[:, :, :, :].rearrange("p c h t -> p c (h t)"), ACT.Copy
                                     ).then_inc(q_hi, 1)
                for j in range(NPG):
                    key_hi(b, j)
                    if values:
                        value_hi(b - 1, j)
                        if j == 1:
                            probs_hi(b - 1)
                act.wait_ge(d_s, b * 4 + 4)
                past(act, pt_tr, b)
                nc.scalar.activation(Pm[:, :], S[:, :], ACT.Exp, bias=smx[:, 0:1], accum_out=sden[:, 0:1]
                                     ).then_inc(s_exp, 1)
            request(0, False)
            request(1, True)
            with act.Fori(2, NREQ) as b:
                request(b, True)
            value_hi(NREQ - 1, 0)
            value_hi(NREQ - 1, 1)
            probs_hi(NREQ - 1)
            for j in range(2, NPG):
                value_hi(NREQ - 1, j)
            act.wait_ge(d_o, 2 * NREQ)
            act.wait_ge(o_ev, 2 * C)
            for b in range(NB):
                for c in range(C):
                    nc.scalar.activation(xhi[:, c, blk(b)], OT[:, c, blk(b)], ACT.Copy).then_inc(o_hi, 1)
            residual(Q_ATTN_OUT, PAIRS_OUT, 3)
            rms_apply(3)
            ffn(Q_FFN1, 4, False)
            for b in range(NB):
                act.wait_ge(n_mm, 4 * NB + b + 1)
                nc.scalar.activation(rs[:, b, :], PS[:, 6 + b % 2, 0:BW], ACT.Sqrt,
                                     bias=epst[:, 0:1], scale=1.0 / D).then_inc(n_sqrt, 1)
            for t in range(NT + 1):
                n = P if t < NT else NS
                act.wait_ge(y_tr, 2 * t + 1)
                past(act, y_st[t % 2], 16 * (t // 2))
                nc.scalar.activation(ytok[0:n, t % 2, 0:512], PS[0:n, 2 * (t % 2), :], ACT.Copy).then_inc(y_ea, 1)
            act.wait_ge(st_out, 32)
            act.wait_ge(out_st2, 16)

        @block.vector
        def _(dve):
            def norm_block(n, b, chunk):
                dve.wait_ge(n_sqrt, n * NB + b + 1)
                nc.vector.reciprocal(rs[:, b, :], rs[:, b, :]).then_inc(n_rec, 1)
                dve.wait_ge(n_rec, n * NB + b + 1)

                def lo_part(c):
                    dve.wait_ge(n_hi, (n * NB + b) * C + c + 1)
                    nc.vector.tensor_tensor(xlo[:, c, blk(b)], tm[:, tmi(b, c), :], xhi[:, c, blk(b)].bitcast(F32),
                                            ALU.subtract).then_inc(n_lo, 1)
                for c in range(C):
                    i = (n * NB + b) * C + c
                    if i >= 3:
                        dve.wait_ge(n_lo, i - 2)
                    chunk(b, c).then_inc(n_tm, 1)
                    if c >= 1:
                        lo_part(c - 1)
                lo_part(C - 1)

            def rms_apply(r, row):
                def chunk(b, c):
                    return nc.vector.scalar_tensor_tensor(
                        tm[:, tmi(b, c), :], X[:, c, blk(b)], par[:, c, row:row + 1], rs[:, b, :], ALU.mult, ALU.mult)
                for b in range(NB):
                    norm_block(NORM_OF_RMS[r], b, chunk)

            def clear_sums(r):
                nc.vector.memset(ssq[:, :, :], 0.0).then_inc(s_zero, 1)
                dve.wait_ge(s_zero, r + 1)

            def residual(q0, n, r, bias=False):
                if r is not None:
                    clear_sums(r)
                with dve.Fori(q0, q0 + n) as q:
                    for s in range(2):
                        for b in range(NB):
                            dve.wait_ge(mm, q * (2 * NB) + (s * NB + b + 1))
                            xs = X[:, ds(q * 2 + (s - 2 * q0), 1), blk(b)].rearrange("p a t -> p (a t)")
                            if bias:
                                bc = par[:, ds(q * 2 + (s - 2 * q0), 1), R_BOUT:R_BOUT + 1].rearrange("p a t -> p (a t)")
                                nc.vector.scalar_tensor_tensor(xs, PS[:, NB * s + b, 0:BW], bc, xs,
                                                               ALU.add, ALU.add).then_inc(ev[s], 1)
                            else:
                                nc.vector.tensor_tensor(xs, PS[:, NB * s + b, 0:BW], xs, ALU.add).then_inc(ev[s], 1)
                        for b in range(NB if r is not None else 0):
                            dve.wait_ge(s_sq, q * (2 * NB) + (r * PIECES - 2 * NB * q0 + s * NB + b + 1))
                            nc.vector.tensor_tensor(ssq[:, b, :], ssq[:, b, :], sq[:, b, :], ALU.add
                                                    ).then_inc(s_ssq, 1)

            def ffn(q, r, gated):
                for gi, g in enumerate(GROUPS):
                    with dve.Fori(q, q + g) as i:
                        for b in range(NB):
                            dve.wait_ge(gate, i * NB + ((gated - q) * NB + b + 1))
                            dve.wait_ge(mm, i * (2 * NB) + (NB + b + 1))
                            nc.vector.tensor_tensor(ht[:, b, :], PS[:, NB + b, 0:BW], ht[:, b, :], ALU.mult
                                                    ).then_inc(ev[1], 1)
                        for b in range(NB):
                            dve.wait_ge(h_hi, i * NB + ((gated - C - q) * NB + b + 1))
                            hx = (slice(None), ds(i - q, 1), blk(b))
                            nc.vector.tensor_tensor(hlo[hx].rearrange("p a t -> p (a t)"), ht[:, b, :],
                                                    hhi[hx].rearrange("p a t -> p (a t)").bitcast(F32),
                                                    ALU.subtract).then_inc(ev[0], 1)
                    q += g
                    gated += g
                    residual(q, PAIRS_OUT, r if gi == len(GROUPS) - 1 else None)
                    q += PAIRS_OUT

            nc.vector.memset(ssq[:, :, :], 0.0).then_inc(s_zero, 1)
            for t in range(NT + 1):
                dve.wait_ge(s_xin[0], t + 1)
                n = P if t < NT else NS
                nc.vector.tensor_copy(X[:, 0:4, t * P:t * P + n],
                                      PS[:, t % 3, 0:4 * n].rearrange("p (c t) -> p c t", t=n)).then_inc(s_xev[0], 1)
            dve.wait_ge(s_zero, 1)
            for i in range(PIECES):
                dve.wait_ge(s_sq, i + 1)
                nc.vector.tensor_tensor(ssq[:, i % NB, :], ssq[:, i % NB, :], sq[:, i % NB, :], ALU.add
                                        ).then_inc(s_ssq, 1)
            dve.wait_ge(s_tr0, 1)
            nc.vector.tensor_copy(par[:, :, :], PS[:, 7, 0:C * NPAR].rearrange("p (c r) -> p c r", r=NPAR)
                                  ).then_inc(s_ev0, 1)
            dve.wait_ge(s_ev0, 1)
            rms_apply(0, R_MIX)
            for n in range(4):
                i, h = n // 2, n % 2
                dve.wait_ge(s_tr0, n + 2)
                nc.vector.tensor_copy(hist[:, 4 * h:4 * h + 4, i * HR:(i + 1) * HR],
                                      PS[:, 6 + n % 2, 0:4 * HR].rearrange("p (c t) -> p c t", t=HR)
                                      ).then_inc(s_ev0, 1)
            dve.wait_ge(s_ev0, 5)
            nc.vector.memset(u[:, 0:HIST], 0.0).then_inc(cv, 1)

            us = u[:, US0:ULEN].rearrange("p (b t) -> p b t", t=HSEG)
            up = uprod[:, :, :].rearrange("p (b t) k -> p b t k", t=TNEW)
            with dve.Fori(0, C) as c:
                n = [0]

                def step(ins):
                    n[0] += 1
                    ins.then_inc(cv, 1)

                def stepped(m):
                    dve.wait_ge(cv, c * KCH + (m + 1))

                step(nc.vector.tensor_copy(wc[:, :], par[:, ds(c, 1), :].rearrange("p a r -> p (a r)")))
                step(nc.vector.tensor_copy(us[:, :, 0:HIST], hist[:, ds(c, 1), :].rearrange(
                    "p a (b t) -> p (a b) t", t=HIST)))
                stepped(1)
                for b in range(NB):
                    dve.wait_ge(gate, c * NB + (b + 1))
                    lo, hi = b * BW, min((b + 1) * BW, SEQ)
                    ins = nc.vector.scalar_tensor_tensor(
                        u[:, HIST + lo:HIST + hi], PS[:, b, 0:hi - lo], wc[:, R_BIN:R_BIN + 1], ht[:, b, 0:hi - lo],
                        ALU.add, ALU.mult)
                    if b == NB - 1:
                        step(ins)
                        ins = nc.vector.scalar_tensor_tensor(
                            us[:, :, HIST:HSEG], PS[:, b, hi - lo:BW].rearrange("p (b t) -> p b t", t=TNEW),
                            wc[:, R_BIN:R_BIN + 1], ht[:, b, hi - lo:BW].rearrange("p (b t) -> p b t", t=TNEW),
                            ALU.add, ALU.mult)
                    ins.then_inc(ev[0], 1)
                dve.wait_ge(ev[0], c * NB + NB)
                step(nc.vector.tensor_copy(utail[:, ds(c, 1), 0:HIST].rearrange("p a t -> p (a t)"),
                                           u[:, SEQ:SEQ + HIST]))
                step(nc.vector.tensor_copy(utail[:, ds(c, 1), HIST:HIST + NS].rearrange(
                    "p a (b t) -> p (a b) t", t=TNEW), us[:, :, HIST:HSEG]))
                step(nc.vector.tensor_scalar(yacc[:, :], u[:, 0:SEQ], wc[:, R_DW:R_DW + 1],
                                             wc[:, R_BDW:R_BDW + 1], ALU.mult, ALU.add))
                for k in range(1, KD):
                    have = n[0]
                    if k <= TNEW:
                        t = k - 1
                        step(nc.vector.tensor_tensor(
                            up[:, :, t, :], us[:, :, t:t + KW],
                            wc[:, R_DW:R_DW + KW].rearrange("p (a k) -> p a k", a=1).broadcast_to([P, NREQ, KW]),
                            ALU.mult))
                    if k == TNEW + 2:
                        step(nc.vector.tensor_reduce(ys[:, :], uprod[:, :, :], AX.X, ALU.add))
                    if k == TNEW + 4:
                        step(nc.vector.tensor_scalar(
                            ycv[:, ds(c, 1), SEQ:T].rearrange("p a t -> p (a t)"), ys[:, :],
                            wc[:, R_BDW:R_BDW + 1], None, ALU.add))
                    stepped(have)
                    step(nc.vector.scalar_tensor_tensor(yacc[:, :], u[:, k:k + SEQ], wc[:, R_DW + k:R_DW + k + 1],
                                                        yacc[:, :], ALU.mult, ALU.add))
                stepped(n[0])
                dve.wait_ge(p_tap, c * (KP - 1) + (KP - 1))
                nc.vector.tensor_tensor(ycv[:, ds(c, 1), 0:SEQ].rearrange("p a t -> p (a t)"), yacc[:, :], yp[:, :],
                                        ALU.add).then_inc(c_done, 1)
                assert n[0] == KCH, n
                dve.wait_ge(c_done, c + 1)
            dve.wait_ge(st_tr, 1)
            nc.vector.tensor_copy(ustate[:, 0:4 * P], PS[0:HIST + NS, 6, :]).then_inc(st_ev, 1)

            for b in range(NB):
                dve.wait_ge(l_mm, b + 1)
                for c in range(C):
                    nc.vector.scalar_tensor_tensor(ycv[:, c, blk(b)], PS[:, b, 0:BW], -1.0 / D, ycv[:, c, blk(b)],
                                                   ALU.mult, ALU.add).then_inc(l_d, 1)
            dve.wait_ge(st_out, 32)

            def centred(b, c):
                return nc.vector.tensor_tensor(tm[:, tmi(b, c), :], ycv[:, c, blk(b)], rs[:, b, :], ALU.mult)
            for b in range(NB):
                norm_block(1, b, centred)
            residual(Q_CONV_OUT, PAIRS_OUT, 1, bias=True)
            rms_apply(1, R_FFN)
            ffn(Q_FFN0, 2, C)
            rms_apply(2, R_MIX + 1)

            def qk_half(q, s, scale, keys, values):
                u = (q - Q_ATTN_IN) * 2 + s
                if values:
                    dve.wait_ge(stg_st[s], 16 * C)
                else:
                    past(dve, stg_st[s], (q - Q_ATTN_IN) * 16)
                if keys:
                    past(dve, kt_tr, ((q - QK) * 2 + (s - 1)) * 2)
                for b in range(NB):
                    dve.wait_ge(mm, q * (2 * NB) + (s * NB + b + 1))
                    if b == NB - 1:
                        nc.vector.tensor_scalar(
                            newqk[:, ds(u, 1), :].rearrange("p a t -> p (a t)"),
                            PS[:, NB * s + b, BW - NS:BW], scale, None, ALU.mult).then_inc(nqk, 1)
                    nc.vector.tensor_scalar(stg[:, s, blk(b)], PS[:, NB * s + b, 0:BW], scale, None,
                                            ALU.mult).then_inc(ev[s], 1)

            def qk_pair(q, scale, keys, values=False):
                for s in range(2):
                    qk_half(q, s, scale, keys, values)

            qk_pair(Q_ATTN_IN, SCALE, False)
            with dve.Fori(Q_ATTN_IN + 1, QK) as q:
                qk_pair(q, SCALE, False)
            nc.vector.memset(wfs[:, :, 2 * H:P].bitcast(F32), 0.0).then_inc(f_lo, 1)
            dve.wait_ge(f_hi, 1)
            nc.vector.tensor_tensor(wfs[:, :, H:2 * H], wfr[:, :, :], wfs[:, :, 0:H].bitcast(F32), ALU.subtract
                                    ).then_inc(f_lo, 1)
            for b in range(NB):
                dve.wait_ge(f_mm, b + 1)
                nc.vector.tensor_copy(zf[:, blk(b)], PS[0:2 * H, 3 + b, 0:BW]).then_inc(f_z, 1)

            qk_half(QK, 0, 1.0, False, False)
            dve.wait_ge(f_mm, NB + 1)
            nc.vector.tensor_tensor(fz[:, :, :], PS[:, 6, 0:(NT + 1) * H].rearrange("p (t h) -> p t h", h=H),
                                    bf[:, :].rearrange("p (a h) -> p a h", a=1).broadcast_to([P, NT + 1, H]),
                                    ALU.add).then_inc(f_z, 1)
            dve.wait_ge(f_z, NB + 1)
            nc.vector.scalar_tensor_tensor(fe[:, :, :], fz[:, :, :], -1.0, fz[:, :, :], ALU.mult, ALU.min
                                           ).then_inc(f_z, 1)
            dve.wait_ge(f_e, 2)
            nc.vector.scalar_tensor_tensor(Lf[:, :, :], fz[:, :, :], 0.0, fe[:, :, :], ALU.min, ALU.subtract
                                           ).then_inc(f_z, 1)
            dve.wait_ge(f_z, NB + 3)
            nc.vector.tensor_copy(Lnew[:, :], Lf[P - NS:P, NT, :]).then_inc(f_z, 1)
            qk_half(QK, 1, 1.0, False, False)
            with dve.Fori(QK + 1, QV) as q:
                qk_pair(q, 1.0, True)
            dve.wait_ge(c_mm, 1)
            nc.vector.tensor_scalar(negc[:, :, :], PS[:, 6, 0:NT * H].rearrange("p (t h) -> p t h", h=H),
                                    -1.0, None, ALU.mult).then_inc(c_neg, 1)
            nc.vector.tensor_tensor(
                NM[:, :, :, :],
                madd[:, :, :].rearrange("p b (a t) -> p b a t", a=1).broadcast_to([NS, NREQ, H, TNEW]),
                PS[0:NS, 6, NT * H:(NT + 1) * H].rearrange("p (a h b) -> p a h b", a=1, b=1).broadcast_to(
                    [NS, NREQ, H, TNEW]), ALU.subtract).then_inc(c_neg, 1)

            qk_pair(QV, 1.0, True, True)
            for half in range(2):
                dve.wait_ge(c_tr, half + 1)
                nc.vector.tensor_copy(negct[:, 512 * half:512 * half + 512], PS[0:H, 6 + half, :]
                                      ).then_inc(c_nc, 1)
            with dve.Fori(QV + 1, Q_ATTN_OUT) as q:
                qk_pair(q, 1.0, True, True)
            dve.wait_ge(x_mm, 1)
            for half in range(2):
                nc.vector.tensor_copy(cbT[:, 512 * half:512 * half + 512], PS[:, 6 + half, :]).then_inc(x_ev, 1)
            dve.wait_ge(nm_tr, 1)
            nc.vector.tensor_copy(NMT[:, :, :], PS[0:H * TNEW, 0, 0:NREQ * NS].rearrange("p (b k) -> p b k", k=NS)
                                  ).then_inc(x_ev, 1)

            nc.vector.memset(qa[DH:DH + 1, :, :], 1.0).then_inc(a_ones, 1)
            dve.wait_ge(out_st, 16 * 5)

            def output(i, base, t, first):
                dve.wait_ge(a_pv, base + (t + 1))
                nc.vector.reciprocal(rden[:, t:t + 1], den[:, t:t + 1]).then_inc(a_rec, 1)
                dve.wait_ge(a_rec, base + (t + 1))
                s, qt = t // NT, t % NT
                if s == 0 and not first:
                    dve.wait_ge(o_tr, i * 2 + (qt // 4 - 1))
                nc.vector.tensor_scalar(on[:, qt, s * DH:(s + 1) * DH], PS[:, 6 + t % 2, 0:DH],
                                        rden[:, t:t + 1], None, ALU.mult).then_inc(a_on, 1)

            def outputs_out(i, half):
                dve.wait_ge(o_tr, i * 2 + (half + 1))
                nc.vector.tensor_copy(OT[:, ds(i, 1), 512 * half:512 * half + 512].rearrange("p a t -> p (a t)"),
                                      PS[:, 7, :]).then_inc(o_ev, 1)

            def prompt_pair(i):
                base = i * NTAU
                first = isinstance(i, int)
                for t in range(NTAU):
                    qt = t % NT
                    dve.wait_ge(a_sc, base + (t + 1))
                    diag = banks(2 * (t % 2), (qt + 1) * P)[:, qt * P:(qt + 1) * P]
                    nc.vector.tensor_tensor(diag, diag, cmask[:, :], ALU.add).then_inc(a_mk, 1)
                    dve.wait_ge(a_mk, base + (t + 1))
                    nc.vector.tensor_reduce(nmx[:, t:t + 1], banks(2 * (t % 2), (qt + 1) * P), AX.X, ALU.max,
                                            negate=True).then_inc(a_max, 1)
                    if t >= 2:
                        output(i, base, t - 2, first)
                    elif not first:
                        output(i - 1, base - NTAU, NTAU + t - 2, False)
                    if not first and t in (0, 2):
                        outputs_out(i - 1, t // 2)
            prompt_pair(0)
            with dve.Fori(1, C) as i:
                prompt_pair(i)
            output(C - 1, (C - 1) * NTAU, NTAU - 2, False)
            outputs_out(C - 1, 0)
            output(C - 1, (C - 1) * NTAU, NTAU - 1, False)
            outputs_out(C - 1, 1)

            def queries(b):
                past(dve, k_sc, b * 5)
                nc.vector.tensor_tensor(
                    qx[:, :, :, :],
                    newqk[:, 0:C, ds(b * TNEW, TNEW)].rearrange("p c (a t) -> p c a t", a=1).broadcast_to(
                        [P, C, H, TNEW]),
                    own[:, :, :].rearrange("p c (h a) -> p c h a", a=1).broadcast_to([P, C, H, TNEW]), ALU.mult
                ).then_inc(d_q, 1)
                dve.wait_ge(q_hi, b + 1)
                nc.vector.tensor_tensor(qs[:, :, 64:P], qx[:, :, :, :].rearrange("p c h t -> p c (h t)"),
                                        qs[:, :, 0:64].bitcast(F32), ALU.subtract).then_inc(d_q, 1)

            def key_lo(b, j):
                g = j // 2
                dve.wait_ge(k_hi, b * NPG + (j + 1))
                part = (slice(None), g % 2, slice(None), slice((j % 2) * P, (j % 2 + 1) * P))
                nc.vector.tensor_tensor(KTl[part], banks(2 * (j % 2), D).rearrange("p (c f) -> p c f", f=P),
                                        KTh[part].bitcast(F32), ALU.subtract).then_inc(k_lo, 1)

            def probs_lo(b):
                dve.wait_ge(p_hi, b + 1)
                nc.vector.tensor_tensor(PTs[:, :, 64:P], PS[:, 2, :].rearrange("p (k c) -> p k c", c=64),
                                        PTs[:, :, 0:64].bitcast(F32), ALU.subtract).then_inc(p_lo, 1)
                nc.vector.tensor_copy(PTn[:, 0:64], PS[0:NS, 3, 0:64]).then_inc(p_lo, 1)
                nc.vector.reciprocal(srd[0:64, :], sden[:, :]).then_inc(d_r, 1)
                dve.wait_ge(d_r, b * 2 + 1)
                nc.vector.tensor_copy(srd[64:P, :], srd[0:64, :]).then_inc(d_r, 1)

            def score_sums(b):
                dve.wait_ge(k_sc, b * 5 + 4)
                dve.wait_ge(cb_ld, b * 16 + 16)
                past(dve, s_exp, b)
                nc.vector.tensor_tensor(S[:, 0:PAST], banks(4, PAST)[64:P, :], cbx[:, :], ALU.add).then_inc(d_s, 1)
                dve.wait_ge(d_s, b * 4 + 1)
                nc.vector.tensor_tensor(S[:, 0:PAST], banks(4, PAST)[0:64, :], S[:, 0:PAST], ALU.add).then_inc(d_s, 1)
                dve.wait_ge(k_sc, b * 5 + 5)
                nc.vector.tensor_tensor(S[:, PAST:PAST + NS], PS[0:64, 3, 0:NS],
                                        NMT[:, ds(b, 1), :].rearrange("p a k -> p (a k)"), ALU.add).then_inc(d_s, 1)
                dve.wait_ge(d_s, b * 4 + 3)
                nc.vector.tensor_reduce(smx[:, :], S[:, :], AX.X, ALU.max, negate=True).then_inc(d_s, 1)

            def sample_out(b):
                dve.wait_ge(p_pv, b + 1)
                past(dve, o_sel, b)
                dve.wait_ge(d_r, b * 2 + 2)
                nc.vector.tensor_scalar(ob[:, :], banks(6, D), srd[:, 0:1], None, ALU.mult).then_inc(d_ob, 1)

            def to_features(b):
                dve.wait_ge(o_sel, b + 1)
                for s in range(2):
                    rows = slice(64 * s, 64 * s + 64)
                    nc.vector.tensor_copy(
                        OT[rows, :, ds(b * TNEW + SEQ, TNEW)],
                        PS[rows, 6, 0:64].rearrange("p (c e) -> p c e", e=8)[:, :, TNEW * s:TNEW * s + TNEW]
                    ).then_inc(d_o, 1)

            def request(b, values, selects):
                queries(b)
                for j in range(NPG):
                    key_lo(b, j)
                    if j == 0 and selects:
                        to_features(b - 2)
                    if j == 1 and values:
                        probs_lo(b - 1)
                score_sums(b)
                if values:
                    sample_out(b - 1)
            dve.wait_ge(a_pv, NTILES)
            dve.wait_ge(cb_st, 16)
            nc.vector.memset(PTn[:, 64:P], 0.0).then_inc(d_z, 1)
            request(0, False, False)
            request(1, True, False)
            with dve.Fori(2, NREQ) as b:
                request(b, True, True)
            to_features(NREQ - 2)
            probs_lo(NREQ - 1)
            sample_out(NREQ - 1)
            to_features(NREQ - 1)
            for b in range(NB):
                for c in range(C):
                    dve.wait_ge(o_hi, b * C + c + 1)
                    nc.vector.tensor_tensor(xlo[:, c, blk(b)], OT[:, c, blk(b)],
                                            xhi[:, c, blk(b)].bitcast(F32), ALU.subtract).then_inc(o_lo, 1)
            residual(Q_ATTN_OUT, PAIRS_OUT, 3)
            rms_apply(3, R_FFN + 1)
            ffn(Q_FFN1, 4, C + FC)
            for b in range(NB):
                dve.wait_ge(n_sqrt, 5 * NB + b + 1)
                nc.vector.reciprocal(rs[:, b, :], rs[:, b, :]).then_inc(n_rec, 1)
                dve.wait_ge(n_rec, 5 * NB + b + 1)
                for c in range(C):
                    nc.vector.scalar_tensor_tensor(yn[:, c, blk(b)], X[:, c, blk(b)], par[:, c, R_FIN:R_FIN + 1],
                                                   rs[:, b, :], ALU.mult, ALU.mult).then_inc(y_n, 1)
            for t in range(NT + 1):
                n = P if t < NT else NS
                dve.wait_ge(y_tr, 2 * t + 2)
                past(dve, y_st[t % 2], 16 * (t // 2))
                nc.vector.tensor_copy(ytok[0:n, t % 2, 512:1024], PS[0:n, 2 * (t % 2) + 1, :]).then_inc(y_ed, 1)


_NAMES = ["x_prompt", "x_sample", "state_conv", "cache_k", "cache_v", "cache_logf", "page_table",
          "norm_mix_g", "norm_ffn_g", "norm_final_g",
          "conv_w_in", "conv_b_in", "conv_w_dw", "conv_b_dw", "conv_ln_g", "conv_ln_b", "conv_w_out", "conv_b_out",
          "attn_w_in", "attn_b_f", "attn_w_out", "ffn_w_gu", "ffn_w_down"]


def _outputs(inputs):
    _, seq, d = inputs["x_prompt"].shape
    nreq, tnew, _ = inputs["x_sample"].shape
    hist = inputs["conv_w_dw"].shape[1] - 1
    h, dh = inputs["cache_k"].shape[3:]
    return [(1, seq, d), (nreq, tnew, d), (1, 1, hist, d), (1, nreq, hist, d),
            (1, 1, seq, h, dh), (1, 1, seq, h, dh), (1, 1, seq, h),
            (1, nreq, tnew, h, dh), (1, nreq, tnew, h, dh), (1, nreq, tnew, h)]


def kernel(**inputs):
    import numpy as np
    import concourse.bacc as bacc
    from concourse.bass_utils import run_bass_kernel_spmd

    nc = bacc.Bacc("TRN2", target_bir_lowering=False, num_devices=1)
    arrays, args = {}, []
    for name in _NAMES:
        a = np.ascontiguousarray(inputs[name])
        arrays[f"in_{name}"] = a
        args.append(nc.dram_tensor(f"in_{name}", a.shape, mybir.dt.from_np(a.dtype), kind="ExternalInput").ap())
    shapes = _outputs(inputs)
    for i, shape in enumerate(shapes):
        args.append(nc.dram_tensor(f"out_{i}", shape, F32, kind="ExternalOutput").ap())
    hybrid_step(nc, *args)
    got = run_bass_kernel_spmd(nc, [arrays], core_ids=[0]).results[0]
    return tuple(got[f"out_{i}"] for i in range(len(shapes)))
```
